# Optimizing a Trainium2 kernel written in Bass

```python
import jax, jax.numpy as jnp
from jax import lax
import numpy as np

D_MODEL = 1024
BATCH = 1
SEQ = 512
DEPTH = 2

GRID_W = 64
CTX_LEN = 256
N_MIXERS = 3
N_MOD = 9
D_FF = 2816
EPS = 1e-6
N_FOURIER_GROUPS = 4
D_CONV = D_MODEL
CONV_K = 31
N_HEADS = 16
HEAD_DIM = D_MODEL // N_HEADS
WIN_R = 8
WIN_C = 16
Q_BLOCK_C = 16
K_BAND_C = 32
N_COL_BLOCKS = GRID_W // Q_BLOCK_C
NEG_INF = -1e30
N_LAYERS_A = len(range(0, DEPTH, N_MIXERS))
N_LAYERS_B = len(range(1, DEPTH, N_MIXERS))
N_LAYERS_C = len(range(2, DEPTH, N_MIXERS))

kernel_name = "hybrid_fnet_conformer_natten_prefix_dit"

def rms_norm(x):
    xf = x.astype(jnp.float32)
    return (xf * lax.rsqrt(jnp.mean(xf * xf, axis=-1, keepdims=True) + EPS)).astype(x.dtype)

def head_rms_norm(t, gain):
    tf = t.astype(jnp.float32)
    return (tf * lax.rsqrt(jnp.mean(tf * tf, axis=-1, keepdims=True) + EPS)).astype(t.dtype) * gain

def modulate(h, shift, scale):
    return h * (1 + scale) + shift

def swiglu(h, w_in, w_out):
    g, u = jnp.split(h @ w_in, 2, axis=-1)
    return (jax.nn.silu(g) * u) @ w_out

def fourier_mix(h, w_out, b_out):
    b, l, d = h.shape
    hg = h.astype(jnp.float32).reshape(b, l, N_FOURIER_GROUPS, d // N_FOURIER_GROUPS)
    f = jnp.fft.fft2(hg, axes=(1, 3), norm="ortho").real
    return f.reshape(b, l, d).astype(h.dtype) @ w_out + b_out

def conformer_conv(h, w_in, b_in, w_dw, b_dw, ln_g, ln_b, w_out, b_out):
    a, g = jnp.split(h @ w_in + b_in, 2, axis=-1)
    u = a * jax.nn.sigmoid(g)
    u = lax.conv_general_dilated(
        u, w_dw[:, None, :], window_strides=(1,),
        padding=[(CONV_K // 2, CONV_K // 2)],
        dimension_numbers=("NWC", "WIO", "NWC"),
        feature_group_count=D_CONV) + b_dw
    uf = u.astype(jnp.float32)
    mu = jnp.mean(uf, axis=-1, keepdims=True)
    var = jnp.mean(jnp.square(uf - mu), axis=-1, keepdims=True)
    u = ((uf - mu) * lax.rsqrt(var + EPS)).astype(u.dtype) * ln_g + ln_b
    return jax.nn.silu(u) @ w_out + b_out

def neighbourhood_attention(a, ac, w_qkv, q_gain, k_gain, rpb, w_o, ctx_out):
    b, l, d = a.shape
    rows = l // GRID_W
    kr = min(WIN_R, rows)
    n_lat = kr * K_BAND_C
    scale = HEAD_DIM ** -0.5
    H, hd, ncb, qbc, kbc = N_HEADS, HEAD_DIM, N_COL_BLOCKS, Q_BLOCK_C, K_BAND_C

    q, k, v = jnp.split(a @ w_qkv, 3, axis=-1)
    q = head_rms_norm(q.reshape(b, l, H, hd), q_gain)
    k = head_rms_norm(k.reshape(b, l, H, hd), k_gain)
    v = v.reshape(b, l, H, hd)
    qc_, kc, vc = jnp.split(ac @ w_qkv, 3, axis=-1)
    n_ctx = ac.shape[1]
    kc = head_rms_norm(kc.reshape(b, n_ctx, H, hd), k_gain)
    vc = vc.reshape(b, n_ctx, H, hd)

    jb = np.arange(ncb)
    band0 = np.clip(jb * qbc - WIN_C // 2, 0, GRID_W - kbc)
    band_cols = band0[:, None] + np.arange(kbc)
    q_cols = jb[:, None] * qbc + np.arange(qbc)
    win0 = np.clip(q_cols - WIN_C // 2, 0, GRID_W - WIN_C)
    kcol = band_cols[:, None, None, :]
    w0 = win0[:, :, None, None]
    col_ok = np.broadcast_to((kcol >= w0) & (kcol < w0 + WIN_C), (ncb, qbc, kr, kbc)).reshape(ncb, qbc, n_lat)
    dc_idx = np.broadcast_to(np.clip(kcol - q_cols[:, :, None, None] + WIN_C - 1, 0, 2 * WIN_C - 2),
                             (ncb, qbc, kr, kbc))

    q_grid = q.reshape(b, rows, ncb, qbc, H, hd)
    k_grid = k.reshape(b, rows, GRID_W, H, hd)
    v_grid = v.reshape(b, rows, GRID_W, H, hd)

    def row_block(r):
        rs = jnp.clip(r - kr // 2, 0, rows - kr)
        q_r = lax.dynamic_index_in_dim(q_grid, r, axis=1, keepdims=False)

        def band(t):
            t = lax.dynamic_slice_in_dim(t, rs, kr, axis=1)[:, :, band_cols]
            return jnp.moveaxis(t, 2, 1).reshape(b, ncb, n_lat, H, hd)

        k_r, v_r = band(k_grid), band(v_grid)
        dr_idx = (rs - r + WIN_R - 1) + jnp.arange(kr)
        bias = rpb[:, dr_idx[None, None, :, None], dc_idx].reshape(H, ncb, qbc, n_lat).astype(jnp.float32)
        s_lat = jnp.einsum('bjqhd,bjnhd->bhjqn', q_r, k_r).astype(jnp.float32) * scale + bias
        s_lat = jnp.where(col_ok, s_lat, NEG_INF)
        s_ctx = jnp.einsum('bjqhd,bchd->bhjqc', q_r, kc).astype(jnp.float32) * scale
        p = jax.nn.softmax(jnp.concatenate([s_lat, s_ctx], axis=-1), axis=-1).astype(v.dtype)
        return (jnp.einsum('bhjqn,bjnhd->bjqhd', p[..., :n_lat], v_r)
                + jnp.einsum('bhjqc,bchd->bjqhd', p[..., n_lat:], vc))

    o = lax.map(row_block, jnp.arange(rows))
    y = jnp.moveaxis(o, 0, 1).reshape(b, l, d) @ w_o

    y_ctx = None
    if ctx_out:
        qc = head_rms_norm(qc_.reshape(b, n_ctx, H, hd), q_gain)
        s = jnp.einsum('bqhd,bkhd->bhqk', qc, kc).astype(jnp.float32) * scale
        pc = jax.nn.softmax(s, axis=-1).astype(vc.dtype)
        y_ctx = jnp.einsum('bhqk,bkhd->bqhd', pc, vc).reshape(b, n_ctx, d) @ w_o
    return y, y_ctx

def setup_inputs(seed: int = 0) -> dict:
    key = jax.random.key(seed)
    ks = jax.random.split(key, 24)
    D = D_MODEL

    def nrm(k, shape, s):
        return jax.random.normal(k, shape, jnp.float32) * s

    return {
        "x": nrm(ks[0], (BATCH, SEQ, D), 1.0),
        "c": nrm(ks[1], (BATCH, D), 1.0),
        "ctx": nrm(ks[2], (BATCH, CTX_LEN, D), 1.0),
        "c_ctx": nrm(ks[3], (D,), 1.0),
        "w_mod": nrm(ks[4], (DEPTH, D, N_MOD * D), 0.5 * D ** -0.5),
        "b_mod": nrm(ks[5], (DEPTH, N_MOD * D), 0.02),
        "w_ff_in": nrm(ks[6], (DEPTH, 2, D, 2 * D_FF), D ** -0.5),
        "w_ff_out": nrm(ks[7], (DEPTH, 2, D_FF, D), D_FF ** -0.5),
        "fnet_w_out": nrm(ks[8], (N_LAYERS_A, D, D), D ** -0.5),
        "fnet_b_out": nrm(ks[9], (N_LAYERS_A, D), 0.02),
        "conv_w_in": nrm(ks[10], (N_LAYERS_B, D, 2 * D_CONV), D ** -0.5),
        "conv_b_in": nrm(ks[11], (N_LAYERS_B, 2 * D_CONV), 0.02),
        "conv_w_dw": nrm(ks[12], (N_LAYERS_B, CONV_K, D_CONV), CONV_K ** -0.5),
        "conv_b_dw": nrm(ks[13], (N_LAYERS_B, D_CONV), 0.02),
        "conv_ln_g": 1.0 + nrm(ks[14], (N_LAYERS_B, D_CONV), 0.02),
        "conv_ln_b": nrm(ks[15], (N_LAYERS_B, D_CONV), 0.02),
        "conv_w_out": nrm(ks[16], (N_LAYERS_B, D_CONV, D), D_CONV ** -0.5),
        "conv_b_out": nrm(ks[17], (N_LAYERS_B, D), 0.02),
        "na_w_qkv": nrm(ks[18], (N_LAYERS_C, D, 3 * D), D ** -0.5),
        "na_q_gain": 1.0 + nrm(ks[19], (N_LAYERS_C, HEAD_DIM), 0.02),
        "na_k_gain": 1.0 + nrm(ks[20], (N_LAYERS_C, HEAD_DIM), 0.02),
        "na_rpb": nrm(ks[21], (N_LAYERS_C, N_HEADS, 2 * WIN_R - 1, 2 * WIN_C - 1), 0.1),
        "na_w_o": nrm(ks[22], (N_LAYERS_C, D, D), D ** -0.5),
    }

def reference(x, c, ctx, c_ctx, w_mod, b_mod, w_ff_in, w_ff_out, fnet_w_out, fnet_b_out,
              conv_w_in, conv_b_in, conv_w_dw, conv_b_dw, conv_ln_g, conv_ln_b, conv_w_out, conv_b_out,
              na_w_qkv, na_q_gain, na_k_gain, na_rpb, na_w_o):
    silu_c = jax.nn.silu(c)
    silu_cc = jax.nn.silu(c_ctx)
    h, hc = x, ctx
    for i in range(DEPTH):
        kind = i % N_MIXERS
        slot = i // N_MIXERS
        ctx_post = i < DEPTH - 1
        ctx_pre = ctx_post or kind == 2
        m = jnp.split((silu_c @ w_mod[i] + b_mod[i])[:, None, :], N_MOD, axis=-1)
        mc = jnp.split((silu_cc @ w_mod[i] + b_mod[i])[None, None, :], N_MOD, axis=-1)

        h = h + 0.5 * m[2] * swiglu(modulate(rms_norm(h), m[0], m[1]), w_ff_in[i, 0], w_ff_out[i, 0])
        if ctx_pre:
            hc = hc + 0.5 * mc[2] * swiglu(modulate(rms_norm(hc), mc[0], mc[1]), w_ff_in[i, 0], w_ff_out[i, 0])

        a = modulate(rms_norm(h), m[3], m[4])
        yc = None
        if kind == 0:
            y = fourier_mix(a, fnet_w_out[slot], fnet_b_out[slot])
            if ctx_post:
                yc = fourier_mix(modulate(rms_norm(hc), mc[3], mc[4]), fnet_w_out[slot], fnet_b_out[slot])
        elif kind == 1:
            cp = (conv_w_in[slot], conv_b_in[slot], conv_w_dw[slot], conv_b_dw[slot],
                  conv_ln_g[slot], conv_ln_b[slot], conv_w_out[slot], conv_b_out[slot])
            y = conformer_conv(a, *cp)
            if ctx_post:
                yc = conformer_conv(modulate(rms_norm(hc), mc[3], mc[4]), *cp)
        else:
            ac = modulate(rms_norm(hc), mc[3], mc[4])
            y, yc = neighbourhood_attention(a, ac, na_w_qkv[slot], na_q_gain[slot], na_k_gain[slot],
                                            na_rpb[slot], na_w_o[slot], ctx_post)
        h = h + m[5] * y
        if ctx_post:
            hc = hc + mc[5] * yc

        h = h + 0.5 * m[8] * swiglu(modulate(rms_norm(h), m[6], m[7]), w_ff_in[i, 1], w_ff_out[i, 1])
        if ctx_post:
            hc = hc + 0.5 * mc[8] * swiglu(modulate(rms_norm(hc), mc[6], mc[7]), w_ff_in[i, 1], w_ff_out[i, 1])
    return h


_drawn_inputs = setup_inputs


def setup_inputs(seed=0):
    import zlib

    import numpy as np

    out = dict(_drawn_inputs(seed))
    spreads = {}
    factors = {'fnet_b_out': 8.0,
     'conv_b_in': 8.0,
     'conv_b_dw': 8.0,
     'conv_ln_g': 8.0,
     'conv_ln_b': 8.0,
     'conv_b_out': 8.0}
    for name, (base, spread) in spreads.items():
        noise = np.random.default_rng([zlib.crc32(name.encode()), seed]).standard_normal(out[name].shape)
        drawn = base * np.exp(spread * noise) if base else spread * noise
        out[name] = __import__('jax').numpy.asarray(drawn.astype(out[name].dtype))
    for name, factor in factors.items():
        out[name] = (out[name] * factor).astype(out[name].dtype)
    return out
```

```python
from contextlib import ExitStack

import numpy as np

import concourse.bass as bass
from concourse import mybir

F32 = mybir.dt.float32
F32R = mybir.dt.float32r
ALU = mybir.AluOpType
ACT = mybir.ActivationFunctionType

P = 128
EPS = 1e-6
N_GROUPS = 4


def hybrid_backbone(nc, x, c, w_mod, b_mod, w_ff_in, w_ff_out, fnet_w_out, fnet_b_out, conv_w_in,
                    conv_b_in, conv_w_dw, conv_b_dw, conv_ln_g, conv_ln_b, conv_w_out, conv_b_out,
                    dft_pair, dft_tail, out):
    T = x.shape[1]
    D = x.shape[2]
    KD = D // P
    TC = T // P
    FF = w_ff_out.shape[2]
    NI = FF // (2 * P)
    TAPS = conv_w_dw.shape[1]
    HALO = TAPS // 2
    NV = 9
    MU = 512
    UC = MU // P
    NMU = NV * D // MU
    GW = D // N_GROUPS
    assert T == 512 and D == 1024 and FF == NI * 2 * P and NI % 2 == 1 and GW == 2 * P

    HEAD = 4
    FNET_UNITS = (NMU - HEAD - 2 - (NI - 1)) + HEAD
    assert FNET_UNITS == N_GROUPS + 2
    FF_UNIT0 = [HEAD, NMU + HEAD, 2 * NMU - 2, None]

    DVE_TAPS = list(range(24))
    POOL_TAPS = list(range(24, TAPS))

    def pool_taps_before(term):
        per = len(POOL_TAPS) - 1
        return term // per * (per + 1) + term % per + 2

    FFA, FNET, FFB, FFC, CONV, FFD = range(6)
    BUF = {FFA: (0, 0, 0)}
    for prev, nxt, used in ((FFA, FNET, (NI, NI, NI)), (FNET, FFB, (3, 2, 2)), (FFB, FFC, (NI, NI, NI)),
                            (FFC, CONV, (NI, NI, NI)), (CONV, FFD, (5, 5, 2))):
        BUF[nxt] = tuple(a + b for a, b in zip(BUF[prev], used))
    FF_PHASE = [FFA, FFB, FFC, FFD]
    PAIR = {FFA: 0, FNET: NI, FFB: NI + 3, FFC: 2 * NI + 3, CONV: 3 * NI + 3, FFD: 3 * NI + 9}
    TAIL = {FFA: 0, FNET: NI, FFB: NI + 1, FFC: 2 * NI + 1, FFD: 3 * NI + 1}
    HB = {"x": 0, FFA: KD}
    for prev, nxt, updates in ((FFA, FNET, NI), (FNET, FFB, 1), (FFB, FFC, NI), (FFC, CONV, NI), (CONV, FFD, 1)):
        HB[nxt] = HB[prev] + KD * updates
    NORM_H = [HB["x"], HB[FNET] - KD, HB[FNET], HB[FFC] - KD, HB[CONV] - KD, None, HB[CONV]]
    WO_ORDER = [4 * q + j + 2 * dd for q in range(2) for j in range(2) for dd in range(2)]
    IN_ORDER = list(range(KD))
    WO_FNET = [(0, 1), (1, 1), (2, 1), (0, 2)]
    WO_CONV = [(2, 0), (0, 4), (1, 4), (2, 1)]

    ctx = ExitStack()
    with ctx:
        def sb(name, shape, dt=F32):
            return ctx.enter_context(nc.sbuf_tensor(name, shape, dt))

        def sem(name):
            return ctx.enter_context(nc.semaphore(name))

        h = sb("h", [P, KD, T])
        a_hi = sb("a_hi", [P, KD, T], F32R)
        a_lo = sb("a_lo", [P, KD, T], F32R)
        p_hi = sb("p_hi", [P, 2, 2, T], F32R)
        p_lo = sb("p_lo", [P, 2, 2, T], F32R)
        w_hi = [sb(f"w_hi{b}", [P, 16, P], F32R) for b in range(3)]
        w_lo = [sb(f"w_lo{b}", [P, 16, P], F32R) for b in range(3)]
        raw_pair = [sb(f"raw_pair{s}", [P, 16, 2, P]) for s in range(2)]
        raw_down = sb("raw_down", [P, 16, P])
        raw_mod = sb("raw_mod", [P, 2, 4, MU])
        mod_acc = sb("mod_acc", [P, MU])
        tmp_a = sb("tmp_a", [P, 2, T])
        tmp_b = sb("tmp_b", [P, 2, T])
        tmp_c = sb("tmp_c", [P, 2, T])
        sq_sum = sb("sq_sum", [P, T])
        u_pad = sb("u_pad", [P, 2, T + 2 * HALO])
        pool_acc = sb("pool_acc", [P, 2, T])
        pool_term = sb("pool_term", [P, 2, T])
        diag = sb("diag", [P, TC, P])
        ident = sb("ident", [P, P])
        ones = sb("ones", [P, P])
        mean_w = sb("mean_w", [P, P])
        mod = sb("mod", [P, 2, NV * KD])
        bmod = sb("bmod", [P, 2, NV * KD])
        vecs = sb("vecs", [P, 64])
        wdw = sb("wdw", [P, KD, TAPS])
        silu_c = sb("silu_c", [P, KD])
        half_gate = sb("half_gate", [P, 4, KD])
        mix_bias = sb("mix_bias", [P, 2, KD])
        tok_std = sb("tok_std", [P, TC])
        tok_rstd = sb("tok_rstd", [P, TC])
        eps_col = sb("eps_col", [P, 1])
        table_dummy = sb("table_dummy", [P, 1])
        vec_rows = tmp_c[0:64, 1, 0:P]
        bmod_rows = tmp_c[0:NV * KD, 0, 0:2 * P].rearrange("k (l p) -> k l p", l=2)
        wdw_rows = tmp_b[0:TAPS].rearrange("t a n -> t (a n)").rearrange("t (k p) -> t k p", p=P)

        y_conv = raw_mod[:].rearrange("p a b n -> p (a b) n")
        y_hi = p_hi[:].rearrange("p a b n -> p (a b) n")
        y_lo = p_lo[:].rearrange("p a b n -> p (a b) n")
        x_rows = raw_mod[:].rearrange("p a b n -> p (a b n)").rearrange("p (t d) -> p t d", t=TC)
        out_rows = [raw_pair[s][:].rearrange("p a b n -> p (a b n)").rearrange("p (t d) -> p t d", t=TC)
                    for s in range(2)]
        head_raw = [raw_pair[s][:].rearrange("p a b n -> p (a b n)").rearrange("p (k n) -> p k n", k=KD)
                    for s in range(2)]
        B_IN, B_DW, LN_G, LN_B, B_OUT, B_FNET, C_COL = 0, 16, 24, 32, 40, 48, 56

        ps = [ctx.enter_context(nc.psum_tensor(f"bank{b}", [P, 512], F32)) for b in range(8)]
        TOK_BANK, RSTD_BANK, MEAN_BANK, MOD_BANK = 4, 5, 6, 7

        s_vec_in = sem("vec_loaded")
        s_x_in = sem("x_loaded")
        s_head_in = [sem(f"head_half_loaded{n}") for n in range(2 * HEAD)]
        s_pair_in = [sem(f"pair_loaded{s}") for s in range(2)]
        s_down_in = sem("down_loaded")
        s_mod_in = [sem(f"mod_half_loaded{n}") for n in range(2)]
        s_out = sem("out_stored")
        s_const = sem("constants_ready")
        s_vec_t = sem("vec_transposed")
        s_vec = sem("vec_ready")
        s_silu_c = sem("silu_c_ready")
        s_take = sem("chunk_for_h_ready")
        s_h = sem("h_chunk_updated")
        s_w_hi = [sem(f"w_hi_ready{b}") for b in range(3)]
        s_w = [sem(f"w_ready{b}") for b in range(3)]
        s_mod_mac = sem("mod_accumulated")
        s_mod_col = sem("mod_columns")
        s_mod = sem("mod_ready")
        s_gate = sem("gate_ready")
        s_gu = sem("gate_up_ready")
        s_silu = sem("silu_ready")
        s_prod = sem("product_ready")
        s_p_hi = sem("p_hi_ready")
        s_p = sem("p_ready")
        s_center = sem("centered_ready")
        s_sq = sem("square_ready")
        s_sq_sum = sem("squares_added")
        s_tok = sem("token_sums")
        s_std = sem("token_std")
        s_rstd = sem("token_rstd")
        s_diag = sem("diag_ready")
        s_rb = sem("rstd_broadcast")
        s_t = sem("normed_ready")
        s_a_hi = sem("a_hi_ready")
        s_a = sem("a_ready")
        s_spec = sem("spectrum_ready")
        s_y_hi = sem("y_hi_ready")
        s_y = sem("y_ready")
        s_seq = sem("sequence_dft_ready")
        s_f_hi = sem("f_hi_ready")
        s_f = sem("f_ready")
        s_bias = sem("mixer_bias_added")
        s_cgu = sem("conv_in_ready")
        s_sig = sem("sigmoid_ready")
        s_u = sem("conv_u_ready")
        s_tap = sem("dve_taps")
        s_pool_tap = sem("pool_taps")
        s_pool_term = sem("pool_terms")
        s_merge = sem("taps_merged")
        s_y_sum = sem("y_summed")
        s_mean = sem("mean_ready")
        s_out_t = sem("out_transposed")
        s_out_row = sem("out_rows_ready")

        block = ctx.enter_context(nc.Block())

        def up_weights(f):
            return w_ff_in[f // 2, f % 2].rearrange("(k p) n -> p k n", p=P)

        def down_weights(f):
            return w_ff_out[f // 2, f % 2].rearrange("(j p) n -> p j n", p=P)

        def layer_unit(unit):
            return unit // NMU, unit % NMU

        @block.sync
        def _(sp):
            def load_pair(pair, cols0, cols1):
                dst = raw_pair[pair % 2][:].rearrange("p (s k) j n -> p s k (j n)", s=2)
                sp.dma_start(dst[:, 0], cols0).then_inc(s_pair_in[pair % 2], 16)
                sp.dma_start(dst[:, 1], cols1).then_inc(s_pair_in[pair % 2], 16)

            def ff_pair(f, i, pair):
                w = up_weights(f)
                load_pair(pair, w[:, :, bass.ds(i * 2 * P, 2 * P)], w[:, :, bass.ds(i * 2 * P + FF, 2 * P)])

            def wo_pair(w, q, pair):
                v = w[0].rearrange("(k p) n -> p k n", p=P)
                load_pair(pair, v[:, :, 4 * q * P:(4 * q + 2) * P], v[:, :, (4 * q + 2) * P:(4 * q + 4) * P])

            def conv_pair(j, pair):
                v = conv_w_in[0].rearrange("(k p) n -> p k n", p=P)
                load_pair(pair, v[:, :, 2 * P * j:2 * P * (j + 1)], v[:, :, D + 2 * P * j:D + 2 * P * (j + 1)])

            def fourier_pair(pair):
                sp.dma_start(raw_pair[pair % 2][:].rearrange("p a j n -> p (a j n)"),
                             dft_pair).then_inc(s_pair_in[pair % 2], 32)

            def ff_down(f, i):
                sp.dma_start(raw_down[:].rearrange("p (j d) n -> p j (d n)", j=2),
                             down_weights(f)[:, bass.ds(i * 2, 2), :]).then_inc(s_down_in, 16)

            def mod_unit(layer, col):
                v = w_mod[layer].rearrange("(k p) n -> p k n", p=P)
                return [v[:, 4 * half:4 * half + 4, bass.ds(col, MU)] for half in range(2)]

            def mod_loads(unit, layer, col):
                for half, src in enumerate(mod_unit(layer, col)):
                    sp.wait_ge(s_mod_mac, unit * 8 - 8 + 4 * (half + 1))
                    sp.dma_start(raw_mod[:, half], src).then_inc(s_mod_in[half], 16)

            sp.dma_start(vec_rows[C_COL:C_COL + 8, :], c.rearrange("b (k p) -> (b k) p", p=P)).then_inc(s_vec_in, 16)
            for col, v in ((B_IN, conv_b_in), (B_DW, conv_b_dw), (LN_G, conv_ln_g), (LN_B, conv_ln_b),
                           (B_OUT, conv_b_out), (B_FNET, fnet_b_out)):
                n = v.shape[1] // P
                sp.dma_start(vec_rows[col:col + n, :], v[0].rearrange("(k p) -> k p", p=P)).then_inc(s_vec_in, 16)
            sp.dma_start(bmod_rows, b_mod.rearrange("l (k p) -> k l p", p=P)).then_inc(s_vec_in, 16)
            sp.dma_start(wdw_rows, conv_w_dw[0].rearrange("t (k p) -> t k p", p=P)).then_inc(s_vec_in, 16)
            for t in range(TC):
                sp.dma_start(x_rows[:, t], x[0, t * P:(t + 1) * P, :]).then_inc(s_x_in, 16)
            for unit in range(HEAD):
                for half, src in enumerate(mod_unit(0, unit * MU)):
                    if unit >= 2:
                        sp.wait_ge(s_mod_mac, (unit - 2) * 8 + 4 * (half + 1))
                    sp.dma_start(head_raw[unit % 2][:, 4 * half:4 * half + 4], src).then_inc(
                        s_head_in[2 * unit + half], 16)
            sp.wait_ge(s_h, KD)
            for half, src in enumerate(mod_unit(0, HEAD * MU)):
                sp.dma_start(raw_mod[:, half], src).then_inc(s_mod_in[half], 16)
            sp.wait_ge(s_mod_mac, 8 * (HEAD - 1))
            ff_pair(0, 0, 0)
            sp.wait_ge(s_mod_mac, 8 * HEAD)
            ff_pair(0, 1, 1)

            def ff_step(f, i, unit, layer, col, load_up):
                ph = FF_PHASE[f]
                sp.wait_ge(s_w[1], BUF[ph][1] + i + 1)
                if isinstance(i, int) and i == 0:
                    sp.wait_ge(s_w[0], BUF[ph][0] + 1)
                load_up()
                if f != 3 or not isinstance(i, int) or i > 0:
                    prior = BUF[ph][2] + i if f != 1 or not isinstance(i, int) or i > 0 else BUF[FNET][2] + 1
                else:
                    prior = BUF[CONV][2]
                if not (f == 0 and isinstance(i, int) and i == 0):
                    sp.wait_ge(s_w[2], prior)
                ff_down(f, i)
                if unit is not None:
                    mod_loads(unit, layer, col)

            def feed_forward(f, next_pairs):
                ph, first = FF_PHASE[f], PAIR[FF_PHASE[f]]
                u0 = FF_UNIT0[f]
                if u0 is not None:
                    layer, j0 = layer_unit(u0)
                    ff_step(f, 0, u0 + 1, layer, (j0 + 1) * MU, lambda: ff_pair(f, 2, first + 2))
                    if f < 2:
                        mod_loads(u0 + 2, layer, (j0 + 2) * MU)
                else:
                    ff_step(f, 0, None, 0, 0, lambda: ff_pair(f, 2, first + 2))
                in_loop = f < 2
                with sp.Fori(0, (NI - 3) // 2) as r:
                    for odd in range(2):
                        i = r * 2 + (1 + odd)
                        if in_loop:
                            ff_step(f, i, i + (u0 + 2), layer, i * MU + (j0 + 2) * MU,
                                    lambda: ff_pair(f, i + 2, first + 3 + odd))
                        else:
                            ff_step(f, i, None, 0, 0, lambda: ff_pair(f, i + 2, first + 3 + odd))
                for n, i in enumerate((NI - 2, NI - 1)):
                    if in_loop:
                        unit = u0 + 2 + i
                        la, j = layer_unit(unit)
                        ff_step(f, i, unit, la, j * MU, next_pairs[n])
                    else:
                        ff_step(f, i, None, 0, 0, next_pairs[n])

            feed_forward(0, [lambda: fourier_pair(PAIR[FNET]), lambda: wo_pair(fnet_w_out, 0, PAIR[FNET] + 1)])

            sp.wait_ge(s_w[2], BUF[FNET][2])
            sp.dma_start(raw_down[:].rearrange("p a n -> p (a n)"), dft_tail).then_inc(s_down_in, 16)
            sp.wait_ge(s_w[1], BUF[FNET][1] + 1)
            wo_pair(fnet_w_out, 1, PAIR[FNET] + 2)
            base = HEAD + 2 + NI - 1
            def ring_load(unit):
                layer, j = layer_unit(unit)
                mod_loads(unit, layer, j * MU)

            for unit in range(base + 1, base + N_GROUPS + 1):
                ring_load(unit)
            sp.wait_ge(s_w[1], BUF[FNET][1] + 2)
            ff_pair(1, 0, PAIR[FFB])
            ring_load(base + N_GROUPS + 1)
            sp.wait_ge(s_w[2], BUF[FNET][2] + 2)
            sp.wait_ge(s_w[0], BUF[FNET][0] + 3)
            ff_pair(1, 1, PAIR[FFB] + 1)
            ring_load(base + N_GROUPS + 2)

            feed_forward(1, [lambda: ff_pair(2, 0, PAIR[FFC]), lambda: ff_pair(2, 1, PAIR[FFC] + 1)])
            feed_forward(2, [lambda: conv_pair(0, PAIR[CONV]), lambda: conv_pair(1, PAIR[CONV] + 1)])

            b0, b1, b2 = BUF[CONV]
            for j in (2, 3):
                sp.wait_ge(s_w[1], b1 + j - 1)
                conv_pair(j, PAIR[CONV] + j)
            for q in range(2):
                sp.wait_ge(s_w[1], b1 + q + 3)
                wo_pair(conv_w_out, q, PAIR[CONV] + 4 + q)
            sp.wait_ge(s_w[2], b2 + 1)
            sp.wait_ge(s_w[0], b0 + 5)
            ff_pair(3, 0, PAIR[FFD])
            sp.wait_ge(s_w[1], b1 + 5)
            sp.wait_ge(s_w[2], b2 + 2)
            ff_pair(3, 1, PAIR[FFD] + 1)

            ff_step(3, 0, None, 0, 0, lambda: ff_pair(3, 2, PAIR[FFD] + 2))
            with sp.Fori(0, (NI - 3) // 2) as r:
                for odd in range(2):
                    i = r * 2 + (1 + odd)
                    ff_step(3, i, None, 0, 0, lambda: ff_pair(3, i + 2, PAIR[FFD] + 3 + odd))
            for i in (NI - 2, NI - 1):
                sp.wait_ge(s_w[2], BUF[FFD][2] + i)
                ff_down(3, i)

            for half in range(2):
                for t in range(TC):
                    sp.wait_ge(s_out_row, half * TC + t + 1)
                    sp.dma_start(out[0, t * P:(t + 1) * P, half * 512:(half + 1) * 512],
                                 out_rows[0][:, t, half * 512:(half + 1) * 512]).then_inc(s_out, 16)
            sp.wait_ge(s_out, 16 * 2 * TC)

        @block.gpsimd
        def _(pool):
            pool.memset(ident[:], 0.0).then_inc(s_const, 1)
            pool.memset(ones[:], 1.0).then_inc(s_const, 1)
            pool.memset(mean_w[:], 1.0 / D).then_inc(s_const, 1)
            pool.memset(eps_col[:], EPS).then_inc(s_const, 1)
            pool.memset(u_pad[:], 0.0).then_inc(s_const, 1)
            pool.wait_ge(s_const, 5)
            pool.affine_select(out=ident[:], in_=ident[:], compare_op=ALU.not_equal, fill=1.0, base=0,
                               pattern=[[-1, P]], channel_multiplier=1).then_inc(s_const, 1)
            terms = adds = 0
            for ch in range(KD):
                acc = pool_acc[:, ch % 2]
                pool.wait_ge(s_u, ch + 1)
                for j, tap in enumerate(POOL_TAPS):
                    src, w = u_pad[:, ch % 2, tap:tap + T], wdw[:, ch, tap:tap + 1]
                    if j == 0:
                        pool.tensor_scalar(acc, src, w, None, ALU.mult).then_inc(s_pool_tap, 1)
                    else:
                        if terms >= 2:
                            pool.wait_ge(s_pool_tap, pool_taps_before(terms - 2))
                        pool.tensor_scalar(pool_term[:, terms % 2], src, w, None, ALU.mult).then_inc(s_pool_term, 1)
                        terms += 1
                        pool.wait_ge(s_pool_term, terms)
                        pool.wait_ge(s_pool_tap, adds)
                        pool.tensor_tensor(acc, acc, pool_term[:, (terms - 1) % 2], ALU.add).then_inc(s_pool_tap, 1)
                    adds += 1

        @block.scalar
        def _(act):
            def pair_hi(b, use, pair, j, loads):
                act.wait_ge(s_pair_in[pair % 2], loads)
                act.activation(w_hi[b][:], raw_pair[pair % 2][:, :, j, :], ACT.Copy).then_inc(s_w_hi[b], 1)

            def down_hi(loads):
                act.wait_ge(s_down_in, loads)
                act.activation(w_hi[2][:], raw_down[:], ACT.Copy).then_inc(s_w_hi[2], 1)

            def pair_loads(pair):
                return 32 * (pair // 2 + 1)

            def squares(n, src, order):
                act.activation(table_dummy[:], eps_col[:], ACT.Sqrt)
                for o, d in enumerate(order):
                    if n == 5:
                        act.wait_ge(s_center, o + 1)
                    else:
                        act.wait_ge(s_h, NORM_H[n] + o + 1)
                    if o >= 2:
                        act.wait_ge(s_sq_sum, (KD - 1) * n + max(o - 3, 0) + 1)
                    act.activation(tmp_a[:, o % 2], src[:, d], ACT.Square).then_inc(s_sq, 1)
                act.wait_ge(s_tok, n + 1)
                act.activation(tok_std[:], ps[TOK_BANK][:, 0:TC], ACT.Sqrt, bias=eps_col[:],
                               scale=1.0 / D).then_inc(s_std, 1)

            def modulated(n, func, scale, bias):
                for k in range(KD):
                    act.wait_ge(s_t, KD * n + k + 1)
                    if k >= 2:
                        act.wait_ge(s_a, KD * n + k - 1)
                    act.activation(tmp_c[:, k % 2], tmp_b[:, k % 2], func, bias=bias[:, k:k + 1],
                                   scale=scale[:, k:k + 1])
                    act.activation(a_hi[:, k], tmp_b[:, k % 2], func, bias=bias[:, k:k + 1],
                                   scale=scale[:, k:k + 1]).then_inc(s_a_hi, 1)

            def rms(n, order, layer, v):
                squares(n, h, order)
                modulated(n, ACT.Identity, mod[:, layer, (v + 1) * KD:(v + 2) * KD],
                          mod[:, layer, v * KD:(v + 1) * KD])

            def ff_step(f, i, down, convert):
                ph, first = FF_PHASE[f], PAIR[FF_PHASE[f]]
                if down is not None:
                    act.wait_ge(s_take, i * KD + (HB[ph] - KD))
                    down_hi(i * 16 + 16 * TAIL[ph])
                for ch in range(2):
                    act.wait_ge(s_gu, i * 2 + (2 * NI * f + ch + 1))
                    act.activation(tmp_a[:, ch], ps[2 * ch][:], ACT.Silu).then_inc(s_silu, 1)
                    act.wait_ge(s_prod, i * 2 + (2 * NI * f + ch + 1))
                    act.activation(p_hi[:, parity[0], ch], tmp_b[:, ch], ACT.Copy).then_inc(s_p_hi, 1)
                    if convert:
                        slot = (first + parity[0] + 1) % 2
                        if isinstance(i, int):
                            loads = 32 * ((first + i + 1) // 2 + 1)
                        else:
                            loads = i * 16 + (32 * ((first + parity[0] + 1) // 2 + 1) - 16 * parity[0])
                        act.wait_ge(s_pair_in[slot], loads)
                        act.activation(w_hi[ch][:], raw_pair[slot][:, :, ch, :], ACT.Copy).then_inc(s_w_hi[ch], 1)

            parity = [0]

            def feed_forward(f, last=False):
                parity[0] = 0
                ff_step(f, 0, None, True)
                if not last:
                    with act.Fori(0, (NI - 1) // 2) as r:
                        for odd in range(2):
                            parity[0] = (1 + odd) % 2
                            i = r * 2 + (1 + odd)
                            ff_step(f, i, i, True)
                else:
                    with act.Fori(0, (NI - 3) // 2) as r:
                        for odd in range(2):
                            parity[0] = (1 + odd) % 2
                            i = r * 2 + (1 + odd)
                            ff_step(f, i, i, True)
                    parity[0] = 1
                    ff_step(f, NI - 2, NI - 2, True)
                    parity[0] = 0
                    ff_step(f, NI - 1, NI - 1, False)
                act.wait_ge(s_take, HB[FF_PHASE[f]] + KD * (NI - 1))
                down_hi(16 * (TAIL[FF_PHASE[f]] + NI))

            act.wait_ge(s_vec, 1)
            act.activation(silu_c[:], vecs[:, C_COL:C_COL + KD], ACT.Silu).then_inc(s_silu_c, 1)
            squares(0, h, IN_ORDER)
            for ch in range(2):
                pair_hi(ch, 0, 0, ch, 32)
            act.wait_ge(s_mod, HEAD)
            modulated(0, ACT.Identity, mod[:, 0, KD:2 * KD], mod[:, 0, 0:KD])
            feed_forward(0)

            b0, b1, b2 = BUF[FNET]
            squares(1, h, IN_ORDER)
            down_hi(16 * (TAIL[FNET] + 1))
            modulated(1, ACT.Identity, mod[:, 0, 4 * KD:5 * KD], mod[:, 0, 3 * KD:4 * KD])
            for g in range(N_GROUPS):
                for t in range(TC):
                    act.wait_ge(s_spec, TC * g + t + 1)
                    act.activation(y_hi[:, t], ps[t][:], ACT.Copy).then_inc(s_y_hi, 1)
                if g == N_GROUPS - 1:
                    pair_hi(0, 1, PAIR[FNET] + 1, 0, pair_loads(PAIR[FNET] + 1))
                for cc in range(2):
                    act.wait_ge(s_seq, 2 * g + cc + 1)
                    act.activation(a_hi[:, 2 * g + cc], ps[4 + cc][:], ACT.Copy).then_inc(s_f_hi, 1)
            pair_hi(1, 1, PAIR[FNET] + 1, 1, pair_loads(PAIR[FNET] + 1))
            pair_hi(2, 1, PAIR[FNET] + 2, 0, pair_loads(PAIR[FNET] + 2))
            act.wait_ge(s_take, HB[FNET] + 2)
            pair_hi(0, 2, PAIR[FNET] + 2, 1, pair_loads(PAIR[FNET] + 2))
            act.wait_ge(s_take, HB[FNET] + 4)
            pair_hi(1, 0, PAIR[FFB], 1, pair_loads(PAIR[FFB]))
            rms_order = WO_ORDER
            squares(2, h, rms_order)
            pair_hi(0, 0, PAIR[FFB], 0, pair_loads(PAIR[FFB]))
            modulated(2, ACT.Identity, mod[:, 0, 7 * KD:8 * KD], mod[:, 0, 6 * KD:7 * KD])
            feed_forward(1)

            rms(3, IN_ORDER, 1, 0)
            feed_forward(2)

            rms(4, IN_ORDER, 1, 3)
            for ch in range(KD):
                act.wait_ge(s_cgu, ch + 1)
                act.activation(tmp_a[:, ch % 2], ps[2 * (ch % 2) + 1][:], ACT.Sigmoid,
                               bias=vecs[:, B_IN + KD + ch:B_IN + KD + ch + 1]).then_inc(s_sig, 1)
                if ch + 2 < KD:
                    pair = PAIR[CONV] + (ch + 2) // 2
                    pair_hi(ch % 2, 0, pair, ch % 2, pair_loads(pair))
            wo_a, wo_b = PAIR[CONV] + 4, PAIR[CONV] + 5
            pair_hi(2, 0, wo_a, 0, pair_loads(wo_a))
            pair_hi(0, 0, wo_a, 1, pair_loads(wo_a))
            pair_hi(1, 0, wo_b, 0, pair_loads(wo_b))
            squares(5, y_conv, IN_ORDER)
            modulated(5, ACT.Silu, vecs[:, LN_G:LN_G + KD], vecs[:, LN_B:LN_B + KD])
            act.wait_ge(s_take, HB[CONV] + 2)
            pair_hi(2, 0, wo_b, 1, pair_loads(wo_b))
            act.wait_ge(s_take, HB[CONV] + 4)
            pair_hi(0, 0, PAIR[FFD], 0, pair_loads(PAIR[FFD]))
            squares(6, h, WO_ORDER)
            pair_hi(1, 0, PAIR[FFD], 1, pair_loads(PAIR[FFD]))
            modulated(6, ACT.Identity, mod[:, 1, 7 * KD:8 * KD], mod[:, 1, 6 * KD:7 * KD])
            feed_forward(3, last=True)
            for n in range(2 * TC):
                if n % 2:
                    act.wait_ge(s_out_t, n + 1)
                    act.wait_ge(s_out_row, n)
                    act.activation(out_rows[0][:, n % TC, (n // TC) * 512:(n // TC + 1) * 512],
                                   ps[n][:], ACT.Copy).then_inc(s_out_row, 1)

        @block.vector
        def _(dve):
            def pair_lo(b, use, pair, j):
                dve.wait_ge(s_w_hi[b], use + 1)
                dve.tensor_tensor(w_lo[b][:], raw_pair[pair % 2][:, :, j, :], w_hi[b][:].bitcast(F32),
                                  ALU.subtract).then_inc(s_w[b], 1)

            def down_lo(use):
                dve.wait_ge(s_w_hi[2], use + 1)
                dve.tensor_tensor(w_lo[2][:], raw_down[:], w_hi[2][:].bitcast(F32),
                                  ALU.subtract).then_inc(s_w[2], 1)

            def mod_mac(unit, half_ready, rows):
                for k in range(KD):
                    if k % 4 == 0:
                        half_ready(k // 4)
                    if k == 0:
                        w_first = rows(k)
                        if not (isinstance(unit, int) and unit == 0):
                            dve.wait_ge(s_mod_col, unit)
                        dve.tensor_scalar(mod_acc[:], w_first, silu_c[:, 0:1], None,
                                          ALU.mult).then_inc(s_mod_mac, 1)
                    else:
                        dve.wait_ge(s_mod_mac, unit * 8 + k)
                        dve.scalar_tensor_tensor(out=mod_acc[:], in0=rows(k), scalar=silu_c[:, k:k + 1],
                                                 in1=mod_acc[:], op0=ALU.mult,
                                                 op1=ALU.add).then_inc(s_mod_mac, 1)

            def mod_half_ready(loads):
                def ready(half):
                    dve.wait_ge(s_mod_in[half], loads)
                return ready

            def ring_rows(k):
                return raw_mod[:, k // 4, k % 4]

            def mod_store(unit, layer, col):
                dve.wait_ge(s_mod_col, unit + 1)
                dve.tensor_tensor(mod[:, layer, bass.ds(col, UC)], ps[MOD_BANK][:, 0:UC],
                                  bmod[:, layer, bass.ds(col, UC)], ALU.add).then_inc(s_mod, 1)

            def ring_unit(unit):
                mod_mac(unit, mod_half_ready(16 * (unit - HEAD + 1)), ring_rows)

            def ring_store(unit):
                layer, j = layer_unit(unit)
                mod_store(unit, layer, j * UC)

            def square_add(n, o):
                if o == 0:
                    return
                dve.wait_ge(s_sq, KD * n + o + 1)
                if o == 1:
                    dve.tensor_tensor(sq_sum[:], tmp_a[:, 0], tmp_a[:, 1], ALU.add).then_inc(s_sq_sum, 1)
                else:
                    dve.wait_ge(s_sq_sum, (KD - 1) * n + o - 1)
                    dve.tensor_tensor(sq_sum[:], sq_sum[:], tmp_a[:, o % 2], ALU.add).then_inc(s_sq_sum, 1)

            def token_rstd(n):
                dve.wait_ge(s_std, n + 1)
                dve.reciprocal(tok_rstd[:], tok_std[:]).then_inc(s_rstd, 1)
                dve.wait_ge(s_rstd, n + 1)
                for t in range(TC):
                    dve.tensor_scalar(diag[:, t], ident[:], tok_rstd[:, t:t + 1], None,
                                      ALU.mult).then_inc(s_diag, 1)

            def normed(n, src):
                def lo(k):
                    dve.wait_ge(s_a_hi, KD * n + k + 1)
                    dve.tensor_tensor(a_lo[:, k], tmp_c[:, k % 2], a_hi[:, k].bitcast(F32),
                                      ALU.subtract).then_inc(s_a, 1)

                dve.wait_ge(s_rb, n + 1)
                for k in range(KD):
                    dve.tensor_tensor(tmp_b[:, k % 2], src[:, k], ps[RSTD_BANK][:], ALU.mult).then_inc(s_t, 1)
                    if k >= 1:
                        lo(k - 1)
                lo(KD - 1)

            def gated(f, i, ch, par):
                dve.wait_ge(s_silu, i * 2 + (2 * NI * f + ch + 1))
                dve.tensor_tensor(tmp_b[:, ch], tmp_a[:, ch], ps[2 * ch + 1][:], ALU.mult).then_inc(s_prod, 1)
                dve.wait_ge(s_p_hi, i * 2 + (2 * NI * f + ch + 1))
                dve.tensor_tensor(p_lo[:, par, ch], tmp_b[:, ch], p_hi[:, par, ch].bitcast(F32),
                                  ALU.subtract).then_inc(s_p, 1)

            def flush(f, done, d):
                dve.wait_ge(s_take, done * KD + (HB[FF_PHASE[f]] + d + 1))
                dve.scalar_tensor_tensor(out=h[:, d], in0=ps[4 + d % 4][:], scalar=half_gate[:, f, d:d + 1],
                                         in1=h[:, d], op0=ALU.mult, op1=ALU.add).then_inc(s_h, 1)

            def ff_step(f, i, par, unit, layer, col, convert):
                ph, first = FF_PHASE[f], PAIR[FF_PHASE[f]]
                down_lo(i + (BUF[ph][2] - 1))
                if unit is not None:
                    mod_mac(unit, mod_half_ready(i * 16 + 16 * (FF_UNIT0[f] - HEAD + 2)), ring_rows)
                slot = (first + par + 1) % 2
                gated(f, i, 0, par)
                if convert:
                    pair_lo(0, i + (BUF[ph][0] + 1), slot, 0)
                gated(f, i, 1, par)
                if unit is not None:
                    mod_store(unit, layer, col)
                for d in range(KD):
                    flush(f, i - 1, d)
                if convert:
                    pair_lo(1, i + (BUF[ph][1] + 1), slot, 1)

            def feed_forward(f, n, last=False):
                ph, first = FF_PHASE[f], PAIR[FF_PHASE[f]]
                u0 = FF_UNIT0[f]
                slot = (first + 1) % 2
                if u0 is not None:
                    layer, j0 = layer_unit(u0)
                    ring_unit(u0)
                gated(f, 0, 0, 0)
                pair_lo(0, BUF[ph][0] + 1, slot, 0)
                if u0 is not None:
                    mod_store(u0, layer, j0 * UC)
                    ring_unit(u0 + 1)
                gated(f, 0, 1, 0)
                pair_lo(1, BUF[ph][1] + 1, slot, 1)
                if u0 is not None:
                    mod_store(u0 + 1, layer, (j0 + 1) * UC)
                la, v = f // 2, 2 if f % 2 == 0 else 8
                dve.wait_ge(s_mod, la * NMU + 2 * v + 2)
                dve.tensor_scalar(half_gate[:, f], mod[:, la, v * KD:(v + 1) * KD], 0.5, None,
                                  ALU.mult).then_inc(s_gate, 1)
                dve.wait_ge(s_gate, f + 1)
                in_loop = f < 2

                def body(i, par, convert):
                    if in_loop:
                        ff_step(f, i, par, i + (u0 + 1), layer, i * UC + (j0 + 1) * UC, convert)
                    else:
                        ff_step(f, i, par, None, 0, 0, convert)

                with dve.Fori(0, (NI - 1) // 2 - (1 if last else 0)) as r:
                    for odd in range(2):
                        body(r * 2 + (1 + odd), (1 + odd) % 2, True)
                if last:
                    body(NI - 2, 1, True)
                    body(NI - 1, 0, False)
                down_lo(BUF[ph][2] + NI - 1)
                for d in range(KD):
                    flush(f, NI - 1, d)
                    if d >= 1 and not last:
                        square_add(n, d - 1)
                if not last:
                    square_add(n, KD - 1)

            def project(n, layer, unit=None):
                for o, d in enumerate(WO_ORDER):
                    dve.wait_ge(s_take, NORM_H[n] + o + 1)
                    dve.scalar_tensor_tensor(out=h[:, d], in0=ps[o % 4][:],
                                             scalar=mod[:, layer, 5 * KD + d:5 * KD + d + 1], in1=h[:, d],
                                             op0=ALU.mult, op1=ALU.add).then_inc(s_h, 1)
                    if o >= 1:
                        square_add(n, o - 1)
                    if unit is not None and o == 1:
                        ring_unit(unit)
                    if unit is not None and o == 3:
                        ring_store(unit)
                        ring_unit(unit + 1)
                    if unit is not None and o == 5:
                        ring_store(unit + 1)
                square_add(n, KD - 1)

            def add_mixer_bias(layer, col):
                dve.tensor_tensor(mix_bias[:, layer], mod[:, layer, 5 * KD:6 * KD], vecs[:, col:col + KD],
                                  ALU.mult).then_inc(s_bias, 1)
                dve.wait_ge(s_bias, (KD + 1) * layer + 1)
                for d in range(KD):
                    dve.tensor_scalar(h[:, d], h[:, d], mix_bias[:, layer, d:d + 1], None,
                                      ALU.add).then_inc(s_bias, 1)
                dve.wait_ge(s_bias, (KD + 1) * (layer + 1))

            dve.wait_ge(s_vec_t, 1)
            dve.tensor_copy(vecs[:], ps[6][:, 0:64]).then_inc(s_vec, 1)
            V = NV * KD
            bm = ps[6][:, 64:64 + 2 * V].rearrange("p (l v k) -> p l v k", l=2, v=NV)
            bmv = bmod[:].rearrange("p l (v k) -> p l v k", v=NV)
            for v in range(NV):
                dve.tensor_scalar(bmv[:, :, v], bm[:, :, v], 1.0 if v % 3 == 1 else 0.0, None,
                                  ALU.add).then_inc(s_vec, 1)
            dve.tensor_copy(wdw[:], ps[6][:, 256:512].rearrange("p (k t) -> p k t", k=KD)[:, :, 0:TAPS]).then_inc(
                s_vec, 1)
            dve.wait_ge(s_vec, NV + 2)
            dve.wait_ge(s_silu_c, 1)
            for d in range(KD):
                dve.wait_ge(s_take, d + 1)
                dve.tensor_copy(h[:, d], ps[d % 4][:]).then_inc(s_h, 1)
                if d >= 1:
                    square_add(0, d - 1)
            square_add(0, KD - 1)
            for unit in range(HEAD):
                def head_ready(half):
                    dve.wait_ge(s_head_in[2 * unit + half], 16)
                mod_mac(unit, head_ready, lambda k: head_raw[unit % 2][:, k])
                if unit == 0:
                    token_rstd(0)
                mod_store(unit, 0, unit * UC)
            for b in range(2):
                pair_lo(b, 0, 0, b)
            normed(0, h)
            feed_forward(0, 1)

            token_rstd(1)
            down_lo(BUF[FNET][2])
            normed(1, h)
            base = HEAD + 2 + NI - 1
            add_mixer_bias(0, B_FNET)
            unit = base
            for g in range(N_GROUPS):
                for t in range(TC):
                    dve.wait_ge(s_y_hi, TC * g + t + 1)
                    dve.tensor_tensor(y_lo[:, t], ps[t][:], y_hi[:, t].bitcast(F32), ALU.subtract).then_inc(s_y, 1)
                if g == N_GROUPS - 1:
                    pair_lo(0, BUF[FNET][0] + 1, PAIR[FNET] + 1, 0)
                ring_unit(unit)
                for cc in range(2):
                    dve.wait_ge(s_f_hi, 2 * g + cc + 1)
                    dve.tensor_tensor(a_lo[:, 2 * g + cc], ps[4 + cc][:], a_hi[:, 2 * g + cc].bitcast(F32),
                                      ALU.subtract).then_inc(s_f, 1)
                ring_store(unit)
                unit += 1
            pair_lo(1, BUF[FNET][1] + 1, PAIR[FNET] + 1, 1)
            pair_lo(2, BUF[FNET][2] + 1, PAIR[FNET] + 2, 0)
            pair_lo(0, BUF[FNET][0] + 2, PAIR[FNET] + 2, 1)
            project(2, 0, unit)
            pair_lo(1, BUF[FFB][1], PAIR[FFB], 1)
            token_rstd(2)
            pair_lo(0, BUF[FFB][0], PAIR[FFB], 0)
            normed(2, h)
            feed_forward(1, 3)
            token_rstd(3)
            normed(3, h)
            feed_forward(2, 4)

            token_rstd(4)
            normed(4, h)
            add_mixer_bias(1, B_OUT)
            taps = 0
            for ch in range(KD):
                slot = ch % 2
                dve.wait_ge(s_sig, ch + 1)
                if ch >= 2:
                    dve.wait_ge(s_pool_tap, len(POOL_TAPS) * (ch - 1))
                dve.scalar_tensor_tensor(out=u_pad[:, slot, HALO:HALO + T], in0=ps[2 * slot][:],
                                         scalar=vecs[:, B_IN + ch:B_IN + ch + 1], in1=tmp_a[:, slot],
                                         op0=ALU.add, op1=ALU.mult).then_inc(s_u, 1)
                if ch + 2 < KD:
                    pair_lo(slot, BUF[CONV][slot] + ch // 2 + 1, PAIR[CONV] + (ch + 2) // 2, slot)
                dve.wait_ge(s_u, ch + 1)
                for j, tap in enumerate(DVE_TAPS):
                    acc, src, w = ps[4 + j % 2][:], u_pad[:, slot, tap:tap + T], wdw[:, ch, tap:tap + 1]
                    if j == 0:
                        dve.tensor_scalar(acc, src, w, vecs[:, B_DW + ch:B_DW + ch + 1], ALU.mult,
                                          ALU.add).then_inc(s_tap, 1)
                    elif j == 1:
                        dve.tensor_scalar(acc, src, w, None, ALU.mult).then_inc(s_tap, 1)
                    else:
                        dve.wait_ge(s_tap, taps - 1)
                        dve.scalar_tensor_tensor(out=acc, in0=src, scalar=w, in1=acc, op0=ALU.mult,
                                                 op1=ALU.add).then_inc(s_tap, 1)
                    taps += 1
                dve.wait_ge(s_tap, taps)
                dve.wait_ge(s_pool_tap, len(POOL_TAPS) * (ch + 1))
                dve.tensor_tensor(y_conv[:, ch], ps[4][:], pool_acc[:, slot], ALU.add).then_inc(s_merge, 1)
                dve.wait_ge(s_merge, 2 * ch + 1)
                dve.tensor_tensor(y_conv[:, ch], ps[5][:], y_conv[:, ch], ALU.add).then_inc(s_merge, 1)
                if ch >= 1:
                    dve.wait_ge(s_merge, 2 * ch + 2)
                    if ch >= 2:
                        dve.wait_ge(s_y_sum, ch - 1)
                    dve.tensor_tensor(sq_sum[:], y_conv[:, 0] if ch == 1 else sq_sum[:], y_conv[:, ch],
                                      ALU.add).then_inc(s_y_sum, 1)
            b0, b1, b2 = BUF[CONV]
            pair_lo(2, b2, PAIR[CONV] + 4, 0)
            dve.wait_ge(s_mean, 1)
            for d in range(KD):
                dve.tensor_tensor(y_conv[:, d], y_conv[:, d], ps[MEAN_BANK][:],
                                  ALU.subtract).then_inc(s_center, 1)
                if d >= 1:
                    square_add(5, d - 1)
            square_add(5, KD - 1)
            token_rstd(5)
            pair_lo(0, b0 + 4, PAIR[CONV] + 4, 1)
            normed(5, y_conv)
            pair_lo(1, b1 + 4, PAIR[CONV] + 5, 0)
            pair_lo(2, b2 + 1, PAIR[CONV] + 5, 1)
            project(6, 1)
            pair_lo(0, BUF[FFD][0], PAIR[FFD], 0)
            token_rstd(6)
            pair_lo(1, BUF[FFD][1], PAIR[FFD], 1)
            normed(6, h)
            feed_forward(3, 7, last=True)
            for n in range(2 * TC):
                if n % 2 == 0:
                    dve.wait_ge(s_out_t, n + 1)
                    if n:
                        dve.wait_ge(s_out_row, n)
                    dve.tensor_copy(out_rows[0][:, n % TC, (n // TC) * 512:(n // TC + 1) * 512],
                                    ps[n][:]).then_inc(s_out_row, 1)

        @block.tensor
        def _(pe):
            def product(bank, wh, wl, xh, xl, start, stop):
                pe.matmul(bank, wh, xh, start=start, stop=False, skip_group_check=True)
                pe.matmul(bank, wh, xl, start=False, stop=False, skip_group_check=True)
                return pe.matmul(bank, wl, xh, start=False, stop=stop, skip_group_check=True)

            def mod_columns(unit):
                if not (isinstance(unit, int) and unit == 0):
                    pe.wait_ge(s_mod, unit)
                pe.wait_ge(s_mod_mac, unit * 8 + 8)
                for j in range(UC):
                    ins = pe.matmul(ps[MOD_BANK][:, j:j + 1], mod_acc[:, j * P:(j + 1) * P], ones[:, 0:1],
                                    start=True, stop=True, skip_group_check=True)
                ins.then_inc(s_mod_col, 1)

            def token_sums(n):
                pe.wait_ge(s_sq_sum, (KD - 1) * (n + 1))
                for t in range(TC):
                    ins = pe.matmul(ps[TOK_BANK][:, t:t + 1], sq_sum[:, t * P:(t + 1) * P], ones[:, 0:1],
                                    start=True, stop=True, skip_group_check=True)
                ins.then_inc(s_tok, 1)

            def spread_rstd(n):
                for t in range(TC):
                    pe.wait_ge(s_diag, TC * n + t + 1)
                    ins = pe.matmul(ps[RSTD_BANK][:, t * P:(t + 1) * P], ones[:], diag[:, t], start=True,
                                    stop=True, skip_group_check=True)
                ins.then_inc(s_rb, 1)

            def in_chunk(b, banks, n, waits_a, done):
                for k in range(KD):
                    if waits_a:
                        pe.wait_ge(s_a, KD * n + k + 1)
                    for s in range(2):
                        ins = product(ps[banks + s][:], w_hi[b][:, s * KD + k], w_lo[b][:, s * KD + k],
                                      a_hi[:, k], a_lo[:, k], k == 0, k == KD - 1)
                ins.then_inc(done, 1)

            def up(f, i, ch, n, waits_a):
                pe.wait_ge(s_w[ch], i + (BUF[FF_PHASE[f]][ch] + 1))
                if not (isinstance(i, int) and i == 0):
                    pe.wait_ge(s_prod, i * 2 + (2 * NI * f + ch - 1))
                in_chunk(ch, 2 * ch, n, waits_a, s_gu)

            def down(f, done, par, unit):
                pe.wait_ge(s_w[2], done + (BUF[FF_PHASE[f]][2] + 1))
                pe.wait_ge(s_p, done * 2 + (2 * NI * f + 2))
                for d in range(KD):
                    if d >= 4:
                        pe.wait_ge(s_h, done * KD + (HB[FF_PHASE[f]] + d - 3))
                    else:
                        pe.wait_ge(s_h, done * KD + (HB[FF_PHASE[f]] + d - 3))
                    if d == 3 and unit is not None:
                        pe.wait_ge(s_mod, unit + 1)
                    for j in range(2):
                        ins = product(ps[4 + d % 4][:], w_hi[2][:, j * KD + d], w_lo[2][:, j * KD + d],
                                      p_hi[:, par, j], p_lo[:, par, j], j == 0, j == 1)
                    ins.then_inc(s_take, 1)

            def feed_forward(f, n):
                u0 = FF_UNIT0[f]
                for ch in range(2):
                    up(f, 0, ch, n, ch == 0)
                    if u0 is not None:
                        mod_columns(u0 + ch)
                with pe.Fori(0, (NI - 1) // 2) as r:
                    for odd in range(2):
                        i = r * 2 + (1 + odd)
                        up(f, i, 0, n, False)
                        up(f, i, 1, n, False)
                        unit = None
                        if f < 2:
                            unit = i + (u0 + 1)
                            pe.wait_ge(s_h, i * KD + (HB[FF_PHASE[f]] - KD))
                            mod_columns(unit)
                        down(f, r * 2 + odd, odd, unit)
                down(f, NI - 1, (NI - 1) % 2, None)

            def project(layer, uses, order_waits, n, unit=None):
                o = 0
                for j, (b, use) in enumerate(uses):
                    pe.wait_ge(s_w[b], BUF[FNET if layer == 0 else CONV][b] + use + 1)
                    for dd in range(2):
                        if o >= 4:
                            pe.wait_ge(s_h, NORM_H[n] + o - 3)
                        for k in range(KD):
                            if o == 0:
                                pe.wait_ge(*order_waits(k))
                            ins = product(ps[o % 4][:], w_hi[b][:, dd * KD + k], w_lo[b][:, dd * KD + k],
                                          a_hi[:, k], a_lo[:, k], k == 0, k == KD - 1)
                        ins.then_inc(s_take, 1)
                        o += 1
                    if unit is not None and j in (1, 2):
                        mod_columns(unit + j - 1)

            pe.wait_ge(s_const, 6)
            pe.wait_ge(s_vec_in, 16 * 9)
            pe.transpose(ps[6][:, 0:64], vec_rows, ident[0:64, 0:64])
            V = NV * KD
            for la in range(2):
                pe.transpose(ps[6][:, 64 + la * V:64 + (la + 1) * V], bmod_rows[:, la], ident[0:V, 0:V])
            for k in range(KD):
                ins = pe.transpose(ps[6][:, 256 + 32 * k:256 + 32 * k + TAPS], wdw_rows[:, k],
                                   ident[0:TAPS, 0:TAPS])
            ins.then_inc(s_vec_t, 1)
            pe.wait_ge(s_x_in, 16 * TC)
            for d in range(KD):
                if d >= 4:
                    pe.wait_ge(s_h, d - 3)
                for t in range(TC):
                    ins = pe.transpose(ps[d % 4][:, t * P:(t + 1) * P], x_rows[:, t, d * P:(d + 1) * P], ident[:])
                ins.then_inc(s_take, 1)
            token_sums(0)
            mod_columns(0)
            spread_rstd(0)
            for unit in range(1, HEAD):
                mod_columns(unit)
            feed_forward(0, 0)

            token_sums(1)
            spread_rstd(1)
            base = HEAD + 2 + NI - 1
            unit = base
            pe.wait_ge(s_w[0], BUF[FNET][0] + 1)
            th = [w[0][:].rearrange("p (z k a) n -> p z k (a n)", z=2, k=2)[:, 0] for w in (w_hi, w_lo)]
            for g in range(N_GROUPS):
                for t in range(TC):
                    for k in range(2):
                        if t == 0:
                            pe.wait_ge(s_a, KD + 2 * g + k + 1)
                        kk = 2 * g + k
                        tok = slice(t * P, (t + 1) * P)
                        ins = product(ps[t][:], a_hi[:, kk, tok], a_lo[:, kk, tok], th[0][:, k], th[1][:, k],
                                      k == 0, k == 1)
                    ins.then_inc(s_spec, 1)
                if g == 0:
                    pe.wait_ge(s_w[1], BUF[FNET][1] + 1)
                    pe.wait_ge(s_w[2], BUF[FNET][2] + 1)
                else:
                    pe.wait_ge(s_f, 2 * g)
                for t in range(TC):
                    pe.wait_ge(s_y, TC * g + t + 1)
                    tabs = [w[1 + t // 2][:].rearrange("p (t s a) n -> p t s (a n)", t=2, s=2)[:, t % 2]
                            for w in (w_hi, w_lo)]
                    for cc in range(2):
                        for s in range(2):
                            ch = slice(s * GW + cc * P, s * GW + (cc + 1) * P)
                            ins = product(ps[4 + cc][:], y_hi[:, t, ch], y_lo[:, t, ch], tabs[0][:, s],
                                          tabs[1][:, s], t == 0 and s == 0, t == TC - 1 and s == 1)
                        if t == TC - 1:
                            ins.then_inc(s_seq, 1)
                mod_columns(unit)
                unit += 1
            project(0, WO_FNET, lambda k: (s_f, k + 1), 2, unit)
            token_sums(2)
            spread_rstd(2)
            feed_forward(1, 2)
            token_sums(3)
            spread_rstd(3)
            feed_forward(2, 3)

            token_sums(4)
            spread_rstd(4)
            for ch in range(KD):
                b = ch % 2
                pe.wait_ge(s_w[b], BUF[CONV][b] + ch // 2 + 1)
                if ch >= 2:
                    pe.wait_ge(s_u, ch - 1)
                in_chunk(b, 2 * b, 4, ch == 0, s_cgu)
            pe.wait_ge(s_y_sum, KD - 1)
            pe.matmul(ps[MEAN_BANK][:], mean_w[:], sq_sum[:], start=True, stop=True).then_inc(s_mean, 1)
            token_sums(5)
            spread_rstd(5)
            project(1, WO_CONV, lambda k: (s_a, KD * 5 + k + 1), 6)
            token_sums(6)
            spread_rstd(6)
            feed_forward(3, 6)

            for n in range(2 * TC):
                if n == 0:
                    pe.wait_ge(s_h, HB[FFD] + KD * NI)
                for j in range(4):
                    d = (n // TC) * 4 + j
                    ins = pe.transpose(ps[n][:, j * P:(j + 1) * P], h[:, d, (n % TC) * P:(n % TC + 1) * P], ident[:])
                ins.then_inc(s_out_t, 1)


def dft_tables(T, D):
    gw = D // N_GROUPS
    kc = np.arange(gw)
    ang = 2 * np.pi * ((kc[:, None] * kc[None, :]) % gw) / gw
    chan = np.concatenate([np.cos(ang), np.sin(ang)], axis=1) / np.sqrt(gw)
    ks = np.arange(T)
    ang = 2 * np.pi * ((ks[:, None] * ks[None, :]) % T) / T
    seq = np.concatenate([np.cos(ang), -np.sin(ang)], axis=1) / np.sqrt(T)
    unit0 = np.zeros((P, 16, P))
    unit0[:, :8] = chan.reshape(2, P, 4, P).transpose(1, 0, 2, 3).reshape(P, 8, P)
    rows = seq.reshape(T // P, P, 2 * T).transpose(1, 0, 2)
    unit1 = rows[:, :2].reshape(P, 16, P)
    pair = np.stack([unit0, unit1], axis=2).reshape(P, -1)
    tail = rows[:, 2:].reshape(P, -1)
    return pair.astype(np.float32), tail.astype(np.float32)


_INS = ["x", "c", "w_mod", "b_mod", "w_ff_in", "w_ff_out", "fnet_w_out", "fnet_b_out", "conv_w_in", "conv_b_in",
        "conv_w_dw", "conv_b_dw", "conv_ln_g", "conv_ln_b", "conv_w_out", "conv_b_out"]


def kernel(**inputs):
    import concourse.bacc as _bacc
    from concourse.bass_utils import run_bass_kernel_spmd as _run

    nc = _bacc.Bacc("TRN2", target_bir_lowering=False, num_devices=1)
    arrays, args = {}, []

    def give(name, a):
        arrays[name] = a
        args.append(nc.dram_tensor(name, a.shape, mybir.dt.from_np(a.dtype), kind="ExternalInput").ap())

    for name in _INS:
        give(f"in_{name}", np.ascontiguousarray(inputs[name]))
    shape = inputs["x"].shape
    pair, tail = dft_tables(shape[1], shape[2])
    give("dft_pair", pair)
    give("dft_tail", tail)
    args.append(nc.dram_tensor("out_h", shape, F32, kind="ExternalOutput").ap())
    hybrid_backbone(nc, *args)
    r = _run(nc, [arrays], core_ids=[0])
    return r.results[0]["out_h"]
```

```python
from contextlib import ExitStack

import numpy as np

import concourse.bass as bass
from concourse import mybir

F32 = mybir.dt.float32
F32R = mybir.dt.float32r
ALU = mybir.AluOpType
ACT = mybir.ActivationFunctionType

P = 128
EPS = 1e-6
N_GROUPS = 4


def hybrid_backbone(nc, x, c, w_mod, b_mod, w_ff_in, w_ff_out, fnet_w_out, fnet_b_out, conv_w_in,
                    conv_b_in, conv_w_dw, conv_b_dw, conv_ln_g, conv_ln_b, conv_w_out, conv_b_out,
                    dft_pair, dft_tail, out):
    T = x.shape[1]
    D = x.shape[2]
    KD = D // P
    TC = T // P
    FF = w_ff_out.shape[2]
    NI = FF // (2 * P)
    TAPS = conv_w_dw.shape[1]
    HALO = TAPS // 2
    NV = 9
    MU = 512
    UC = MU // P
    NMU = NV * D // MU
    GW = D // N_GROUPS
    assert T == 512 and D == 1024 and FF == NI * 2 * P and NI % 2 == 1 and GW == 2 * P

    HEAD = 4
    ROWS = 2 * NMU
    HEAD_ROW = ROWS - HEAD
    FNET_UNITS = (NMU - HEAD - 2 - (NI - 1)) + HEAD
    assert FNET_UNITS == N_GROUPS + 2
    FF_UNIT0 = [HEAD, NMU + HEAD, 2 * NMU - 2, None]

    NE = 6
    SIGMOID_EARLY = 3
    SPLIT = [(NE, 11)] * (KD - 2) + [(10, 9), (15, 6)]
    PE_TAPS = [list(range(e)) for e, _ in SPLIT]
    POOL_TAPS = [list(range(e, e + p)) for e, p in SPLIT]
    DVE_TAPS = [list(range(e + p, TAPS)) for e, p in SPLIT]
    assert sum(e - NE for e, _ in SPLIT) <= 16

    def before(ch, taps, less=0):
        return sum(len(t) - less for t in taps[:ch])

    TERMS = 4

    FFA, FNET, FFB, FFC, CONV, FFD = range(6)
    FF_PHASE = [FFA, FFB, FFC, FFD]
    seen = [0, 0, 0]

    def place(b, n=1):
        seen[b] += n
        return b, seen[b] - n

    UP, DOWN, DOWN_LAST, FIRST = {}, {}, {}, {}
    WO_UNITS = {}
    x_, y_, z_ = 0, 1, 2
    FIRST[FFA] = [place(x_), place(y_)]
    for ph, f in ((FFA, 0), (FNET, None), (FFB, 1), (FFC, 2), (CONV, None), (FFD, 3)):
        nxt = ph + 1
        if f is not None:
            place(x_, NI - 1), place(y_, NI - 1)
            UP[f] = FIRST[ph]
            DOWN[f] = place(z_, NI - 1)
            DOWN_LAST[f] = place(x_)
            x_, y_, z_ = y_, z_, x_
            if ph != FFD:
                FIRST[nxt] = [place(x_), place(y_)]
        elif ph == FNET:
            TABLE_TAIL = place(z_)
            WO_UNITS[ph] = [place(x_), place(y_), place(z_), place(x_)]
            x_, y_, z_ = y_, z_, x_
            FIRST[nxt] = [place(x_), place(y_)]
        else:
            EXTRA_TAPS_BUF = z_
            CONV_UNITS = FIRST[ph] + [place((x_, y_, z_)[ch % 3]) for ch in range(2, KD)]
            WO_UNITS[ph] = [place(z_), place(x_), place(y_), place(z_)]
            FIRST[nxt] = [place(x_), place(y_)]
    PAIR = {FFA: 0, FNET: NI, FFB: NI + 3, FFC: 2 * NI + 3, CONV: 3 * NI + 3, FFD: 3 * NI + 9}
    TAIL = {FFA: 0, FNET: NI, FFB: NI + 1, FFC: 2 * NI + 1, FFD: 3 * NI + 1}
    HB = {"x": 0, FFA: KD}
    for prev, nxt, updates in ((FFA, FNET, NI), (FNET, FFB, 1), (FFB, FFC, NI), (FFC, CONV, NI), (CONV, FFD, 1)):
        HB[nxt] = HB[prev] + KD * updates
    NORM_H = [HB["x"], HB[FNET] - KD, HB[FNET], HB[FFC] - KD, HB[CONV] - KD, None, HB[CONV]]
    MOD_CALLS = [(0, 2, 0), (2, 4, HEAD), (4, NI + 3, HEAD + 2), (NI + 3, NMU + 2, NI + 5),
                 (NMU + 2, 2 * NMU - 4, NMU + HEAD), (2 * NMU - 4, 2 * NMU - 2, 2 * NMU - 2)]
    MOD_T_BANK = [0, 6, 0, 0, 0, 0]
    GATE_MOD = [3, 5, 6, 7]
    ADDS = KD - 1
    WO_ORDER = [4 * q + j + 2 * dd for q in range(2) for j in range(2) for dd in range(2)]
    IN_ORDER = list(range(KD))

    ctx = ExitStack()
    with ctx:
        def sb(name, shape, dt=F32):
            return ctx.enter_context(nc.sbuf_tensor(name, shape, dt))

        def sem(name):
            return ctx.enter_context(nc.semaphore(name))

        h = sb("h", [P, KD, T])
        a_hi = sb("a_hi", [P, KD, T], F32R)
        a_lo = sb("a_lo", [P, KD, T], F32R)
        p_hi = sb("p_hi", [P, 2, 2, T], F32R)
        p_lo = sb("p_lo", [P, 2, 2, T], F32R)
        w_hi = [sb(f"w_hi{b}", [P, 16, P], F32R) for b in range(3)]
        w_lo = [sb(f"w_lo{b}", [P, 16, P], F32R) for b in range(3)]
        raw_pair = [sb(f"raw_pair{s}", [P, 16, 2, P]) for s in range(2)]
        raw_down = sb("raw_down", [P, 16, P])
        raw_mod = sb("raw_mod", [P, 2, 4, MU])
        mod_acc = sb("mod_acc", [P, MU])
        mod_acc_hi = sb("mod_acc_hi", [P, MU], F32R)
        mod_acc_lo = sb("mod_acc_lo", [P, MU], F32R)
        tmp_a = sb("tmp_a", [P, 2, T])
        tmp_b = sb("tmp_b", [P, 2, T])
        tmp_c = sb("tmp_c", [P, 2, T])
        sq_sum = sb("sq_sum", [P, T])
        u_pad = sb("u_pad", [P, 3, T + 2 * HALO])
        odd_tap_hi = sb("odd_tap_hi", [P, NE, P], F32R)
        odd_tap_lo = sb("odd_tap_lo", [P, NE, P], F32R)
        ident = sb("ident", [P, P])
        ones = sb("ones", [P, P])
        ones_r = sb("ones_r", [P, ROWS], F32R)
        mod_rows = sb("mod_rows", [ROWS, MU])
        mean_w = sb("mean_w", [P, P])
        mod = sb("mod", [P, 2, NV * KD])
        bmod = sb("bmod", [P, 2, NV * KD])
        vecs = sb("vecs", [P, 64])
        wdw = sb("wdw", [P, KD, TAPS])
        wdw_lo = sb("wdw_lo", [P, KD, TAPS])
        silu_c = sb("silu_c", [P, KD])
        half_gate = sb("half_gate", [P, 4, KD])
        mix_bias = sb("mix_bias", [P, 2, KD])
        tok_std = sb("tok_std", [P, TC])
        tok_rstd = sb("tok_rstd", [P, TC])
        eps_col = sb("eps_col", [P, 1])
        table_dummy = sb("table_dummy", [P, 1])
        vec_rows = tmp_c[0:64, 1, 0:P]
        bmod_rows = tmp_c[0:NV * KD, 0, 0:2 * P].rearrange("k (l p) -> k l p", l=2)
        wdw_rows = raw_down[0:TAPS, 0:KD]

        y_conv = raw_mod[:].rearrange("p a b n -> p (a b) n")
        y_hi = p_hi[:].rearrange("p a b n -> p (a b) n")
        y_lo = p_lo[:].rearrange("p a b n -> p (a b) n")
        u_hi = p_hi[:].rearrange("p a b n -> p a (b n)")[:, :, 0:T + 2 * HALO]
        u_lo = p_lo[:].rearrange("p a b n -> p a (b n)")[:, :, 0:T + 2 * HALO]
        even_tap = [p[:].rearrange("p a b n -> p a (b n)")[:, :, 2 * T - NE // 2 * P:].rearrange(
            "p a (j n) -> p a j n", n=P) for p in (p_hi, p_lo)]
        wdw_hi = odd_tap_hi[:].rearrange("p j n -> p (j n)")[:, 0:KD * TAPS].rearrange("p (k t) -> p k t", k=KD)
        pool_acc = tmp_c
        pool_term = raw_down[:].rearrange("p a n -> p (a n)").rearrange("p (s n) -> p s n", s=TERMS)
        diag = tmp_b[:, 0].rearrange("p (t n) -> p t n", t=TC)
        x_rows = raw_mod[:].rearrange("p a b n -> p (a b n)").rearrange("p (t d) -> p t d", t=TC)
        out_rows = [raw_pair[s][:].rearrange("p a b n -> p (a b n)").rearrange("p (t d) -> p t d", t=TC)
                    for s in range(2)]
        slot_rows = [raw_pair[s][:].rearrange("p a b n -> p (a b n)").rearrange("p (k n) -> p k n", k=KD)
                     for s in range(2)]
        head_rows = [slot_rows[1], slot_rows[1], slot_rows[0], raw_mod[:].rearrange("p a b n -> p (a b) n")]
        C_COL, B_IN, B_DW, LN_G, LN_B, B_OUT, B_FNET = 0, 8, 24, 32, 40, 48, 56

        ps = [ctx.enter_context(nc.psum_tensor(f"bank{b}", [P, 512], F32)) for b in range(8)]
        TOK_BANK, RSTD_BANK, MEAN_BANK, MOD_BANK = 4, 5, 6, 7
        HEAD_BANK = {2: 2, 3: 3}
        SEQ_BANKS = [(4, 6)] * (N_GROUPS - 1) + [(1, 2)]

        s_c_in = sem("c_loaded")
        s_vec_in = sem("vec_loaded")
        s_x_in = sem("x_loaded")
        s_head_in = [sem(f"head_half_loaded{n}") for n in range(2 * HEAD)]
        s_pair_in = [sem(f"pair_loaded{s}") for s in range(2)]
        s_down_in = sem("down_loaded")
        s_mod_in = [sem(f"mod_half_loaded{n}") for n in range(2)]
        s_out = sem("out_stored")
        s_const = sem("constants_ready")
        s_c_t = sem("c_transposed")
        s_vec_t = sem("vec_transposed")
        s_vec = sem("vec_ready")
        s_wdw = sem("wdw_split_ready")
        s_silu_c = sem("silu_c_ready")
        s_take = sem("chunk_for_h_ready")
        s_h = sem("h_chunk_updated")
        s_w_hi = [sem(f"w_hi_ready{b}") for b in range(3)]
        s_w = [sem(f"w_ready{b}") for b in range(3)]
        s_mod_mac = sem("mod_accumulated")
        s_head_sum = sem("head_summed")
        s_head_row = sem("head_rows_updated")
        s_mod_hi = sem("mod_hi_ready")
        s_mod_split = sem("mod_split_ready")
        s_mod_sum = sem("mod_summed")
        s_mod_row = sem("mod_rows_updated")
        s_mod_t = sem("mod_transposed")
        s_mod = sem("mod_ready")
        s_gate = sem("gate_ready")
        s_gu = sem("gate_up_ready")
        s_silu = sem("silu_ready")
        s_prod = sem("product_ready")
        s_p_hi = sem("p_hi_ready")
        s_p = sem("p_ready")
        s_center = sem("centered_ready")
        s_sq = sem("square_ready")
        s_sq_sum = sem("squares_added")
        s_tok = sem("token_sums")
        s_std = sem("token_std")
        s_rstd = sem("token_rstd")
        s_diag = sem("diag_ready")
        s_rb = sem("rstd_broadcast")
        s_t = sem("normed_ready")
        s_a_hi = sem("a_hi_ready")
        s_a_full = sem("a_full_ready")
        s_a = sem("a_ready")
        s_spec = sem("spectrum_ready")
        s_y_hi = sem("y_hi_ready")
        s_y = sem("y_ready")
        s_seq = sem("sequence_dft_ready")
        s_f_hi = sem("f_hi_ready")
        s_f = sem("f_ready")
        s_bias = sem("mixer_bias_added")
        s_cgu = sem("conv_in_ready")
        s_sig = sem("sigmoid_ready")
        s_u = sem("conv_u_ready")
        s_tap = sem("dve_taps")
        s_pool_tap = sem("pool_taps")
        s_term = sem("terms_ready")
        s_diag_tap = sem("tap_matrices_ready")
        s_u_hi = sem("conv_u_hi_ready")
        s_u_lo = sem("conv_u_lo_ready")
        s_pe_tap = sem("pe_taps")
        s_merge = sem("taps_merged")
        s_y_sum = sem("y_summed")
        s_mean = sem("mean_ready")
        s_out_t = sem("out_transposed")
        s_out_row = sem("out_rows_ready")

        block = ctx.enter_context(nc.Block())

        def up_weights(f):
            return w_ff_in[f // 2, f % 2].rearrange("(k p) n -> p k n", p=P)

        def down_weights(f):
            return w_ff_out[f // 2, f % 2].rearrange("(j p) n -> p j n", p=P)

        def tap_matrix(ch, j):
            extra = [len(t) - NE for t in PE_TAPS]
            if j < extra[ch]:
                n = sum(extra[:ch]) + j
                return w_hi[EXTRA_TAPS_BUF][:, n], w_lo[EXTRA_TAPS_BUF][:, n]
            j -= extra[ch]
            if ch % 2:
                return odd_tap_hi[:, j], odd_tap_lo[:, j]
            return [p[:, j // (NE // 2), j % (NE // 2)] for p in even_tap]

        def layer_unit(unit):
            return unit // NMU, unit % NMU

        @block.sync
        def _(sp):
            def load_pair(pair, cols0, cols1):
                dst = raw_pair[pair % 2][:].rearrange("p (s k) j n -> p s k (j n)", s=2)
                sp.dma_start(dst[:, 0], cols0).then_inc(s_pair_in[pair % 2], 16)
                sp.dma_start(dst[:, 1], cols1).then_inc(s_pair_in[pair % 2], 16)

            def ff_pair(f, i, pair):
                w = up_weights(f)
                load_pair(pair, w[:, :, bass.ds(i * 2 * P, 2 * P)], w[:, :, bass.ds(i * 2 * P + FF, 2 * P)])

            def wo_pair(w, q, pair):
                v = w[0].rearrange("(k p) n -> p k n", p=P)
                load_pair(pair, v[:, :, 4 * q * P:(4 * q + 2) * P], v[:, :, (4 * q + 2) * P:(4 * q + 4) * P])

            def conv_pair(j, pair):
                v = conv_w_in[0].rearrange("(k p) n -> p k n", p=P)
                load_pair(pair, v[:, :, 2 * P * j:2 * P * (j + 1)], v[:, :, D + 2 * P * j:D + 2 * P * (j + 1)])

            def fourier_pair(pair):
                sp.dma_start(raw_pair[pair % 2][:].rearrange("p a j n -> p (a j n)"),
                             dft_pair).then_inc(s_pair_in[pair % 2], 32)

            def ff_down(f, i):
                sp.dma_start(raw_down[:].rearrange("p (j d) n -> p j (d n)", j=2),
                             down_weights(f)[:, bass.ds(i * 2, 2), :]).then_inc(s_down_in, 16)

            def mod_unit(layer, col):
                v = w_mod[layer].rearrange("(k p) n -> p k n", p=P)
                return [v[:, 4 * half:4 * half + 4, bass.ds(col, MU)] for half in range(2)]

            def mod_loads(unit, layer, col):
                for half, src in enumerate(mod_unit(layer, col)):
                    sp.wait_ge(s_mod_mac, unit * 8 - 24 + 4 * (half + 1))
                    sp.dma_start(raw_mod[:, half], src).then_inc(s_mod_in[half], 16)

            for t in range(TC):
                sp.dma_start(x_rows[:, t], x[0, t * P:(t + 1) * P, :]).then_inc(s_x_in, 16)

            def head_load(unit):
                for half, src in enumerate(mod_unit(0, unit * MU)):
                    sp.dma_start(head_rows[unit][:, 4 * half:4 * half + 4], src).then_inc(
                        s_head_in[2 * unit + half], 16)

            head_load(0)
            head_load(2)
            sp.wait_ge(s_h, KD)
            head_load(3)
            sp.wait_ge(s_mod_mac, KD)
            head_load(1)
            sp.wait_ge(s_head_sum, 1)
            ff_pair(0, 0, 0)
            sp.wait_ge(s_head_sum, 2)
            for half, src in enumerate(mod_unit(0, HEAD * MU)):
                sp.dma_start(raw_mod[:, half], src).then_inc(s_mod_in[half], 16)
            sp.wait_ge(s_mod_mac, 2 * KD)
            ff_pair(0, 1, 1)

            def converted(unit):
                sp.wait_ge(s_w[unit[0]], unit[1] + 1)

            def ff_step(f, i, unit, layer, col, load_up):
                if load_up is not None:
                    sp.wait_ge(s_w[UP[f][1][0]], i + (UP[f][1][1] + 1))
                    load_up()
                if not isinstance(i, int) or i > 0:
                    sp.wait_ge(s_w[DOWN[f][0]], i + DOWN[f][1])
                elif f == 3:
                    sp.wait_ge(s_pool_tap, before(KD, POOL_TAPS, 1))
                elif f > 0:
                    converted((None, TABLE_TAIL, DOWN_LAST[1])[f])
                ff_down(f, i)
                if unit is not None:
                    mod_loads(unit, layer, col)

            def feed_forward(f, next_pairs):
                first = PAIR[FF_PHASE[f]]
                u0 = FF_UNIT0[f]
                if u0 is not None:
                    layer, j0 = layer_unit(u0)
                    ff_step(f, 0, u0 + 1, layer, (j0 + 1) * MU, lambda: ff_pair(f, 2, first + 2))
                    if f < 2:
                        mod_loads(u0 + 2, layer, (j0 + 2) * MU)
                else:
                    ff_step(f, 0, None, 0, 0, lambda: ff_pair(f, 2, first + 2))
                in_loop = f < 2
                with sp.Fori(0, (NI - 3) // 2) as r:
                    for odd in range(2):
                        i = r * 2 + (1 + odd)
                        if in_loop:
                            ff_step(f, i, i + (u0 + 2), layer, i * MU + (j0 + 2) * MU,
                                    lambda: ff_pair(f, i + 2, first + 3 + odd))
                        else:
                            ff_step(f, i, None, 0, 0, lambda: ff_pair(f, i + 2, first + 3 + odd))
                for n, i in enumerate((NI - 2, NI - 1)):
                    load_up = next_pairs[n] if next_pairs else None
                    if in_loop:
                        unit = u0 + 2 + i
                        la, j = layer_unit(unit)
                        ff_step(f, i, unit, la, j * MU, load_up)
                    else:
                        ff_step(f, i, None, 0, 0, load_up)

            feed_forward(0, [lambda: fourier_pair(PAIR[FNET]), lambda: wo_pair(fnet_w_out, 0, PAIR[FNET] + 1)])

            converted(DOWN_LAST[0])
            sp.dma_start(raw_down[:].rearrange("p a n -> p (a n)"), dft_tail).then_inc(s_down_in, 16)
            converted(FIRST[FNET][0])
            converted(FIRST[FNET][1])
            wo_pair(fnet_w_out, 1, PAIR[FNET] + 2)
            base = HEAD + 2 + NI - 1

            def ring_load(unit):
                layer, j = layer_unit(unit)
                mod_loads(unit, layer, j * MU)

            for unit in range(base + 1, base + N_GROUPS + 1):
                ring_load(unit)
            converted(WO_UNITS[FNET][0])
            converted(WO_UNITS[FNET][1])
            ff_pair(1, 0, PAIR[FFB])
            ring_load(base + N_GROUPS + 1)
            converted(WO_UNITS[FNET][2])
            converted(WO_UNITS[FNET][3])
            ff_pair(1, 1, PAIR[FFB] + 1)
            ring_load(base + N_GROUPS + 2)

            feed_forward(1, [lambda: ff_pair(2, 0, PAIR[FFC]), lambda: ff_pair(2, 1, PAIR[FFC] + 1)])
            feed_forward(2, [lambda: conv_pair(0, PAIR[CONV]), lambda: conv_pair(1, PAIR[CONV] + 1)])

            def conv_converted(ch):
                converted(CONV_UNITS[ch])

            for j in (2, 3):
                conv_converted(2 * j - 4)
                conv_converted(2 * j - 3)
                conv_pair(j, PAIR[CONV] + j)
            for q in range(2):
                conv_converted(2 * q + 4)
                conv_converted(2 * q + 5)
                wo_pair(conv_w_out, q, PAIR[CONV] + 4 + q)
            for q in range(2):
                converted(WO_UNITS[CONV][2 * q])
                converted(WO_UNITS[CONV][2 * q + 1])
                ff_pair(3, q, PAIR[FFD] + q)
            feed_forward(3, None)

            for half in range(2):
                for t in range(TC):
                    sp.wait_ge(s_out_row, half * TC + t + 1)
                    sp.dma_start(out[0, t * P:(t + 1) * P, half * 512:(half + 1) * 512],
                                 out_rows[0][:, t, half * 512:(half + 1) * 512]).then_inc(s_out, 16)
            sp.wait_ge(s_out, 16 * 2 * TC)

        @block.gpsimd
        def _(pool):
            pool.memset(ident[:], 0.0).then_inc(s_const, 1)
            pool.memset(ones[:], 1.0).then_inc(s_const, 1)
            pool.memset(mean_w[:], 1.0 / D).then_inc(s_const, 1)
            pool.memset(eps_col[:], EPS).then_inc(s_const, 1)
            pool.memset(u_pad[:], 0.0).then_inc(s_const, 1)
            pool.memset(ones_r[:].bitcast(F32), 1.0).then_inc(s_const, 1)
            pool.memset(mod_rows[:], 0.0).then_inc(s_const, 1)
            pool.wait_ge(s_const, 7)
            pool.affine_select(out=ident[:], in_=ident[:], compare_op=ALU.not_equal, fill=1.0, base=0,
                               pattern=[[-1, P]], channel_multiplier=1).then_inc(s_const, 1)
            adds = 0
            for ch in range(KD):
                acc = pool_acc[:, ch % 2]
                for j in range(len(POOL_TAPS[ch]) - 1):
                    term = before(ch, POOL_TAPS) + j + 1
                    pool.wait_ge(s_term, term + 1)
                    if j == 0:
                        if ch >= 2:
                            pool.wait_ge(s_tap, before(ch - 2, DVE_TAPS) + 2)
                        pool.tensor_tensor(acc, pool_term[:, (term - 1) % TERMS], pool_term[:, term % TERMS],
                                           ALU.add).then_inc(s_pool_tap, 1)
                    else:
                        pool.wait_ge(s_pool_tap, adds)
                        pool.tensor_tensor(acc, acc, pool_term[:, term % TERMS], ALU.add).then_inc(s_pool_tap, 1)
                    adds += 1

        @block.scalar
        def _(act):
            def pair_hi(unit, pair, j):
                b = unit[0]
                act.wait_ge(s_pair_in[pair % 2], 32 * (pair // 2 + 1))
                act.activation(w_hi[b][:], raw_pair[pair % 2][:, :, j, :], ACT.Copy).then_inc(s_w_hi[b], 1)

            def down_hi(b, loads):
                act.wait_ge(s_down_in, loads)
                act.activation(w_hi[b][:], raw_down[:], ACT.Copy).then_inc(s_w_hi[b], 1)

            def mod_hi(unit, sum_before=False):
                act.wait_ge(s_mod_mac, unit * 8 + 8)
                if sum_before:
                    act.wait_ge(s_mod_sum, unit)
                act.activation(mod_acc_hi[:], mod_acc[:], ACT.Copy).then_inc(s_mod_hi, 1)

            def squares(n, src, order, after=()):
                act.activation(table_dummy[:], eps_col[:], ACT.Sqrt)
                for o, d in enumerate(order):
                    if n == 5:
                        act.wait_ge(s_center, o + 1)
                    else:
                        act.wait_ge(s_h, NORM_H[n] + o + 1)
                    if o >= 2:
                        act.wait_ge(s_sq_sum, ADDS * n + max(o - 2, 1))
                    act.activation(tmp_a[:, o % 2], src[:, d], ACT.Square).then_inc(s_sq, 1)
                    for at, work in after:
                        if at == o:
                            work()
                act.wait_ge(s_tok, n + 1)
                act.activation(tok_std[:], ps[TOK_BANK][:, 0:TC], ACT.Sqrt, bias=eps_col[:],
                               scale=1.0 / D).then_inc(s_std, 1)

            def modulated(n, func, scale, bias, after=()):
                for k in range(KD):
                    act.wait_ge(s_t, KD * n + k + 1)
                    act.activation(a_hi[:, k], tmp_b[:, k % 2], func, bias=bias[:, k:k + 1],
                                   scale=scale[:, k:k + 1]).then_inc(s_a_hi, 1)
                    if k >= 2:
                        act.wait_ge(s_a, KD * n + k - 1)
                    act.activation(tmp_c[:, k % 2], tmp_b[:, k % 2], func, bias=bias[:, k:k + 1],
                                   scale=scale[:, k:k + 1]).then_inc(s_a_full, 1)
                    for at, work in after:
                        if at == k:
                            work()

            def rms(n, order, layer, v, among_squares=(), among_chunks=()):
                squares(n, h, order, among_squares)
                modulated(n, ACT.Identity, mod[:, layer, (v + 1) * KD:(v + 2) * KD],
                          mod[:, layer, v * KD:(v + 1) * KD], among_chunks)

            def gated(f, i, ch, par):
                act.wait_ge(s_gu, i * 2 + (2 * NI * f + ch + 1))
                act.activation(tmp_a[:, ch], ps[2 * ch][:], ACT.Silu).then_inc(s_silu, 1)
                act.wait_ge(s_prod, i * 2 + (2 * NI * f + ch + 1))
                act.activation(p_hi[:, par, ch], tmp_b[:, ch], ACT.Copy).then_inc(s_p_hi, 1)

            def next_hi(f, i, ch, par):
                pair = PAIR[FF_PHASE[f]] + par + 1
                act.wait_ge(s_pair_in[pair % 2], (i - par) * 16 + 32 * (pair // 2 + 1))
                b = UP[f][ch][0]
                act.activation(w_hi[b][:], raw_pair[pair % 2][:, :, ch, :], ACT.Copy).then_inc(s_w_hi[b], 1)

            def ff_step(f, i, par, unit, last_step, next_unit):
                if not isinstance(i, int) or i > 0:
                    act.wait_ge(s_take, i * KD + (HB[FF_PHASE[f]] - KD))
                    down_hi(DOWN[f][0], i * 16 + 16 * TAIL[FF_PHASE[f]])
                sum_first = isinstance(i, int) and i == 1
                if unit is not None and sum_first:
                    mod_hi(unit, sum_before=True)
                gated(f, i, 0, par)
                if last_step:
                    down_hi(DOWN_LAST[f][0], 16 * (TAIL[FF_PHASE[f]] + NI))
                else:
                    next_hi(f, i, 0, par)
                if unit is not None and not sum_first:
                    mod_hi(unit)
                gated(f, i, 1, par)
                if not last_step:
                    next_hi(f, i, 1, par)
                elif next_unit is not None:
                    pair_hi(next_unit[0], next_unit[1], 0)

            def feed_forward(f, next_unit):
                u0 = FF_UNIT0[f]
                act.activation(table_dummy[:], eps_col[:], ACT.Silu)
                if u0 is not None:
                    mod_hi(u0 - 2)
                gated(f, 0, 0, 0)
                next_hi(f, 0, 0, 0)
                gated(f, 0, 1, 0)
                next_hi(f, 0, 1, 0)
                if u0 is not None:
                    mod_hi(u0 - 1, sum_before=True)

                def step(i, par):
                    ff_step(f, i, par, i + (u0 - 1) if f < 2 else None, isinstance(i, int) and i == NI - 1,
                            next_unit)

                step(1, 1)
                with act.Fori(0, (NI - 3) // 2) as r:
                    for odd in range(2):
                        step(r * 2 + (2 + odd), odd)
                step(NI - 1, 0)

            act.dma_start(vec_rows[C_COL:C_COL + KD, :], c.rearrange("b (k p) -> (b k) p", p=P)).then_inc(s_c_in, 16)
            for col, v in ((B_IN, conv_b_in), (B_DW, conv_b_dw), (LN_G, conv_ln_g), (LN_B, conv_ln_b),
                           (B_OUT, conv_b_out), (B_FNET, fnet_b_out)):
                n = v.shape[1] // P
                act.dma_start(vec_rows[col:col + n, :], v[0].rearrange("(k p) -> k p", p=P)).then_inc(s_vec_in, 16)
            act.dma_start(bmod_rows, b_mod.rearrange("l (k p) -> k l p", p=P)).then_inc(s_vec_in, 16)
            act.dma_start(wdw_rows, conv_w_dw[0].rearrange("t (k p) -> t k p", p=P)).then_inc(s_vec_in, 16)

            act.wait_ge(s_c_t, 1)
            act.activation(silu_c[:], ps[MOD_BANK][:, C_COL:C_COL + KD], ACT.Silu).then_inc(s_silu_c, 1)
            squares(0, h, IN_ORDER, [(KD - 1, lambda: mod_hi(0))])
            mod_hi(1)
            pair_hi(FIRST[FFA][0], 0, 0)
            act.wait_ge(s_mod, 2)
            modulated(0, ACT.Identity, mod[:, 0, KD:2 * KD], mod[:, 0, 0:KD],
                      [(4, lambda: pair_hi(FIRST[FFA][1], 0, 1))])
            feed_forward(0, (FIRST[FNET][0], PAIR[FNET]))

            def spectrum_hi(g):
                for t in range(TC):
                    act.wait_ge(s_spec, TC * g + t + 1)
                    if g > 0:
                        act.wait_ge(s_seq, TC * (g - 1) + t + 1)
                    act.activation(y_hi[:, t], ps[t][:], ACT.Copy).then_inc(s_y_hi, 1)

            squares(1, h, IN_ORDER, [(0, lambda: pair_hi(FIRST[FNET][1], PAIR[FNET], 1))])
            modulated(1, ACT.Identity, mod[:, 0, 4 * KD:5 * KD], mod[:, 0, 3 * KD:4 * KD],
                      [(5, lambda: spectrum_hi(0)),
                       (6, lambda: down_hi(TABLE_TAIL[0], 16 * (TAIL[FNET] + 1)))])
            base = HEAD + 2 + NI - 1
            for g in range(N_GROUPS):
                if g + 1 < N_GROUPS:
                    spectrum_hi(g + 1)
                for cc in range(2):
                    act.wait_ge(s_seq, TC * (g + 1))
                    act.activation(a_hi[:, 2 * g + cc], ps[SEQ_BANKS[g][cc]][:], ACT.Copy).then_inc(s_f_hi, 1)
                if g == N_GROUPS - 2:
                    pair_hi(WO_UNITS[FNET][0], PAIR[FNET] + 1, 0)
                if g < N_GROUPS - 2:
                    mod_hi(base + g - 2)
            pair_hi(WO_UNITS[FNET][1], PAIR[FNET] + 1, 1)
            mod_hi(base + N_GROUPS - 4)
            pair_hi(WO_UNITS[FNET][2], PAIR[FNET] + 2, 0)
            act.wait_ge(s_take, HB[FNET] + 2)
            pair_hi(WO_UNITS[FNET][3], PAIR[FNET] + 2, 1)
            mod_hi(base + N_GROUPS - 3, sum_before=True)
            act.wait_ge(s_take, HB[FNET] + 4)
            pair_hi(FIRST[FFB][0], PAIR[FFB], 0)
            rms(2, WO_ORDER, 0, 6, [(2, lambda: mod_hi(base + N_GROUPS - 2, sum_before=True)),
                                    (4, lambda: mod_hi(base + N_GROUPS - 1, sum_before=True)),
                                    (5, lambda: pair_hi(FIRST[FFB][1], PAIR[FFB], 1))])
            feed_forward(1, (FIRST[FFC][0], PAIR[FFC]))

            rms(3, IN_ORDER, 1, 0, [(0, lambda: pair_hi(FIRST[FFC][1], PAIR[FFC], 1))])
            feed_forward(2, (FIRST[CONV][0], PAIR[CONV]))

            rms(4, IN_ORDER, 1, 3, [(0, lambda: pair_hi(FIRST[CONV][1], PAIR[CONV], 1))])

            def tap_matrices(ch, j):
                if ch >= 2 and j >= len(PE_TAPS[ch]) - NE:
                    act.wait_ge(s_pe_tap, ch - 1)
                tap_hi, tap_lo = tap_matrix(ch, j)
                tap = PE_TAPS[ch][j]
                act.activation(tap_hi, ident[:], ACT.Identity, scale=wdw[:, ch, tap:tap + 1])
                act.activation(tap_lo, ident[:], ACT.Identity,
                               scale=wdw_lo[:, ch, tap:tap + 1]).then_inc(s_diag_tap, 1)

            def sigmoid(ch):
                act.wait_ge(s_cgu, ch + 1)
                act.activation(tmp_a[:, ch % 2], ps[2 * (ch % 2) + 1][:], ACT.Sigmoid,
                               bias=vecs[:, B_IN + KD + ch:B_IN + KD + ch + 1]).then_inc(s_sig, 1)

            act.wait_ge(s_wdw, 2)
            for j in range(NE):
                tap_matrices(0, j)
            sigmoid(0)
            for ch in range(KD):
                act.wait_ge(s_u, ch + 1)
                if ch >= 2:
                    act.wait_ge(s_pe_tap, ch - 1)
                act.activation(u_hi[:, ch % 2], u_pad[:, ch % 3], ACT.Copy).then_inc(s_u_hi, 1)
                if ch + 2 < KD:
                    pair_hi(CONV_UNITS[ch + 2], PAIR[CONV] + (ch + 2) // 2, ch % 2)
                matrices = len(PE_TAPS[ch + 1]) if ch + 1 < KD else 0
                products = len(POOL_TAPS[ch])
                per = -(-matrices // (products - 1))
                begin = products - -(-matrices // per) if matrices else products
                for j, tap in enumerate(POOL_TAPS[ch]):
                    term = before(ch, POOL_TAPS) + j
                    if term >= TERMS:
                        old = term - TERMS
                        c0 = max(k for k in range(ch + 1) if before(k, POOL_TAPS) <= old)
                        act.wait_ge(s_pool_tap, before(c0, POOL_TAPS, 1) + max(old - before(c0, POOL_TAPS), 1))
                    act.activation(pool_term[:, term % TERMS], u_pad[:, ch % 3, tap:tap + T], ACT.Identity,
                                   scale=wdw[:, ch, tap:tap + 1],
                                   bias=vecs[:, B_DW + ch:B_DW + ch + 1] if j == 0 else 0.0).then_inc(s_term, 1)
                    if j >= begin:
                        for m in range((j - begin) * per, min((j - begin + 1) * per, matrices)):
                            tap_matrices(ch + 1, m)
                    if j == products - 1 - (SIGMOID_EARLY if ch == KD - 2 else 0) and ch + 1 < KD:
                        sigmoid(ch + 1)
            units = WO_UNITS[CONV]
            for j in (1, 2, 0):
                if j == 0:
                    act.wait_ge(s_pe_tap, KD)
                pair_hi(units[j], PAIR[CONV] + 4 + j // 2, j % 2)
            squares(5, y_conv, IN_ORDER)
            modulated(5, ACT.Silu, vecs[:, LN_G:LN_G + KD], vecs[:, LN_B:LN_B + KD])
            act.wait_ge(s_take, HB[CONV] + 2)
            pair_hi(units[3], PAIR[CONV] + 5, 1)
            act.wait_ge(s_take, HB[CONV] + 4)
            pair_hi(FIRST[FFD][0], PAIR[FFD], 0)
            rms(6, WO_ORDER, 1, 6, [(5, lambda: pair_hi(FIRST[FFD][1], PAIR[FFD], 1))])
            feed_forward(3, None)
            for n in range(2 * TC):
                if n % 2:
                    act.wait_ge(s_out_t, n + 1)
                    act.wait_ge(s_out_row, n)
                    act.activation(out_rows[0][:, n % TC, (n // TC) * 512:(n // TC + 1) * 512],
                                   ps[n][:], ACT.Copy).then_inc(s_out_row, 1)

        @block.vector
        def _(dve):
            def pair_lo(unit, pair, j):
                b, use = unit
                dve.wait_ge(s_w_hi[b], use + 1)
                dve.tensor_tensor(w_lo[b][:], raw_pair[pair % 2][:, :, j, :], w_hi[b][:].bitcast(F32),
                                  ALU.subtract).then_inc(s_w[b], 1)

            def down_lo(unit):
                b, use = unit
                dve.wait_ge(s_w_hi[b], use + 1)
                dve.tensor_tensor(w_lo[b][:], raw_down[:], w_hi[b][:].bitcast(F32),
                                  ALU.subtract).then_inc(s_w[b], 1)

            def mod_mac(unit, half_ready, rows):
                for k in range(KD):
                    if k % 4 == 0:
                        half_ready(k // 4)
                    if k == 0:
                        if isinstance(unit, int) and unit > 0:
                            dve.wait_ge(s_mod_split, unit)
                        dve.tensor_scalar(mod_acc[:], rows(k), silu_c[:, 0:1], None,
                                          ALU.mult).then_inc(s_mod_mac, 1)
                    else:
                        dve.wait_ge(s_mod_mac, unit * 8 + k)
                        dve.scalar_tensor_tensor(out=mod_acc[:], in0=rows(k), scalar=silu_c[:, k:k + 1],
                                                 in1=mod_acc[:], op0=ALU.mult,
                                                 op1=ALU.add).then_inc(s_mod_mac, 1)

            def mod_lo(unit):
                dve.wait_ge(s_mod_hi, unit + 1)
                dve.tensor_tensor(mod_acc_lo[:], mod_acc[:], mod_acc_hi[:].bitcast(F32),
                                  ALU.subtract).then_inc(s_mod_split, 1)

            def mod_half_ready(loads):
                def ready(half):
                    dve.wait_ge(s_mod_in[half], loads)
                return ready

            def ring_rows(k):
                return raw_mod[:, k // 4, k % 4]

            def mod_row(unit):
                dve.wait_ge(s_mod_sum, unit + 1)
                if not isinstance(unit, int) or unit > 0:
                    dve.wait_ge(s_mod_row, unit)
                dve.scalar_tensor_tensor(out=mod_rows[:], in0=ps[MOD_BANK][0:ROWS, :],
                                         scalar=ident[0:ROWS, bass.ds(unit, 1)], in1=mod_rows[:],
                                         op0=ALU.mult, op1=ALU.add).then_inc(s_mod_row, 1)

            def mod_columns(call):
                dve.wait_ge(s_mod_t, call + 1)
                row_range_columns(call, *MOD_CALLS[call])
                if call == 0:
                    row_range_columns(call, ROWS - 2, ROWS, 2)

            def row_range_columns(call, row0, row1, unit0):
                n = row1 - row0
                cols = [v[:].rearrange("p l n -> p (l n)")[:, unit0 * UC:(unit0 + n) * UC].rearrange(
                    "p (u c) -> p c u", c=UC) for v in (mod, bmod)]
                src = ps[MOD_T_BANK[call]][:, 0:UC * ROWS].rearrange("p (c u) -> p c u", c=UC)[:, :, row0:row1]
                dve.tensor_tensor(cols[0], src, cols[1], ALU.add).then_inc(s_mod, 1)

            def ring_unit(unit):
                mod_mac(unit - 2, mod_half_ready(16 * (unit - HEAD + 1)), ring_rows)
                mod_lo(unit - 2)

            def square_add(n, o):
                if o == 0:
                    return
                dve.wait_ge(s_sq, KD * n + o + 1)
                if o == 1:
                    dve.tensor_tensor(sq_sum[:], tmp_a[:, 0], tmp_a[:, 1], ALU.add).then_inc(s_sq_sum, 1)
                else:
                    dve.wait_ge(s_sq_sum, ADDS * n + o - 1)
                    dve.tensor_tensor(sq_sum[:], sq_sum[:], tmp_a[:, o % 2], ALU.add).then_inc(s_sq_sum, 1)

            def token_rstd(n):
                dve.wait_ge(s_std, n + 1)
                dve.reciprocal(tok_rstd[:], tok_std[:]).then_inc(s_rstd, 1)
                dve.wait_ge(s_rstd, n + 1)
                for t in range(TC):
                    dve.tensor_scalar(diag[:, t], ident[:], tok_rstd[:, t:t + 1], None,
                                      ALU.mult).then_inc(s_diag, 1)

            def normed(n, src, after=()):
                def lo(k):
                    dve.wait_ge(s_a_full, KD * n + k + 1)
                    dve.tensor_tensor(a_lo[:, k], tmp_c[:, k % 2], a_hi[:, k].bitcast(F32),
                                      ALU.subtract).then_inc(s_a, 1)
                    for at, work in after:
                        if at == k:
                            work()

                dve.wait_ge(s_rb, n + 1)
                for k in range(KD):
                    if k >= 2:
                        dve.wait_ge(s_a_full, KD * n + k - 1)
                    dve.tensor_tensor(tmp_b[:, k % 2], src[:, k], ps[RSTD_BANK][:], ALU.mult).then_inc(s_t, 1)
                    if k >= 1:
                        lo(k - 1)
                lo(KD - 1)

            def gated(f, i, ch, par):
                dve.wait_ge(s_silu, i * 2 + (2 * NI * f + ch + 1))
                dve.tensor_tensor(tmp_b[:, ch], tmp_a[:, ch], ps[2 * ch + 1][:], ALU.mult).then_inc(s_prod, 1)
                dve.wait_ge(s_p_hi, i * 2 + (2 * NI * f + ch + 1))
                dve.tensor_tensor(p_lo[:, par, ch], tmp_b[:, ch], p_hi[:, par, ch].bitcast(F32),
                                  ALU.subtract).then_inc(s_p, 1)

            def flush(f, done, d):
                dve.wait_ge(s_take, done * KD + (HB[FF_PHASE[f]] + d + 1))
                dve.scalar_tensor_tensor(out=h[:, d], in0=ps[4 + d % 4][:], scalar=half_gate[:, f, d:d + 1],
                                         in1=h[:, d], op0=ALU.mult, op1=ALU.add).then_inc(s_h, 1)

            def next_lo(f, i, ch, par):
                b, use = UP[f][ch]
                pair_lo((b, i + (use + 1)), PAIR[FF_PHASE[f]] + par + 1, ch)

            def ff_step(f, i, par, unit, last_step, next_unit, after_down):
                down_lo((DOWN[f][0], i + (DOWN[f][1] - 1)))
                if after_down is not None:
                    after_down()
                if unit is not None:
                    mod_mac(unit, mod_half_ready(i * 16 + 16 * (FF_UNIT0[f] - HEAD + 2)), ring_rows)
                if unit is not None and after_down is not None:
                    mod_lo(unit)
                gated(f, i, 0, par)
                if last_step:
                    down_lo(DOWN_LAST[f])
                else:
                    next_lo(f, i, 0, par)
                if unit is not None and after_down is None:
                    mod_lo(unit)
                gated(f, i, 1, par)
                if unit is not None:
                    mod_row(unit)
                for d in range(KD):
                    flush(f, i - 1, d)
                if not last_step:
                    next_lo(f, i, 1, par)
                elif next_unit is not None:
                    pair_lo(next_unit[0], next_unit[1], 0)

            def feed_forward(f, n, next_unit):
                u0 = FF_UNIT0[f]
                if u0 is not None:
                    ring_unit(u0)
                gated(f, 0, 0, 0)
                next_lo(f, 0, 0, 0)
                if u0 is not None:
                    mod_mac(u0 - 1, mod_half_ready(16 * (u0 + 2 - HEAD)), ring_rows)
                gated(f, 0, 1, 0)
                next_lo(f, 0, 1, 0)
                if u0 is not None:
                    mod_row(u0 - 2)
                    mod_lo(u0 - 1)

                def gate_columns():
                    if u0 is not None:
                        mod_row(u0 - 1)
                    if f == 0:
                        mod_columns(1)
                    la, v = f // 2, 2 if f % 2 == 0 else 8
                    dve.wait_ge(s_mod, GATE_MOD[f])
                    dve.tensor_scalar(half_gate[:, f], mod[:, la, v * KD:(v + 1) * KD], 0.5, None,
                                      ALU.mult).then_inc(s_gate, 1)
                    dve.wait_ge(s_gate, f + 1)

                def step(i, par, last_step, after_down=None):
                    ff_step(f, i, par, i + (u0 - 1) if f < 2 else None, last_step, next_unit, after_down)

                step(1, 1, False, gate_columns)
                with dve.Fori(0, (NI - 3) // 2) as r:
                    for odd in range(2):
                        step(r * 2 + (2 + odd), odd, False)
                step(NI - 1, 0, True)
                for d in range(KD):
                    flush(f, NI - 1, d)
                    if d >= 1 and n is not None:
                        square_add(n, d - 1)
                if n is not None:
                    square_add(n, KD - 1)

            def project(n, layer, after, unit=None):
                for o, d in enumerate(WO_ORDER):
                    dve.wait_ge(s_take, NORM_H[n] + o + 1)
                    dve.scalar_tensor_tensor(out=h[:, d], in0=ps[o % 4][:],
                                             scalar=mod[:, layer, 5 * KD + d:5 * KD + d + 1], in1=h[:, d],
                                             op0=ALU.mult, op1=ALU.add).then_inc(s_h, 1)
                    if o >= 1:
                        square_add(n, o - 1)
                    for at, work in after:
                        if at == o:
                            work()
                    if unit is not None and o in (1, 3, 5):
                        m = unit - 4 + o // 2
                        mod_row(m)
                        mod_lo(m + 1)
                        if o < 5:
                            mod_mac(m + 2, mod_half_ready(16 * (m + 5 - HEAD)), ring_rows)
                if unit is not None:
                    mod_row(unit - 1)
                square_add(n, KD - 1)

            def add_mixer_bias(layer, col):
                dve.wait_ge(s_mod, (4, 6)[layer])
                dve.tensor_tensor(mix_bias[:, layer], mod[:, layer, 5 * KD:6 * KD], vecs[:, col:col + KD],
                                  ALU.mult).then_inc(s_bias, 1)
                dve.wait_ge(s_bias, (KD + 1) * layer + 1)
                for d in range(KD):
                    dve.tensor_scalar(h[:, d], h[:, d], mix_bias[:, layer, d:d + 1], None,
                                      ALU.add).then_inc(s_bias, 1)
                dve.wait_ge(s_bias, (KD + 1) * (layer + 1))

            for d in range(KD):
                dve.wait_ge(s_take, d + 1)
                dve.tensor_copy(h[:, d], ps[d % 4][:]).then_inc(s_h, 1)
                if d >= 1:
                    square_add(0, d - 1)
            square_add(0, KD - 1)

            def head_mac(unit):
                def ready(half):
                    dve.wait_ge(s_head_in[2 * unit + half], 16)
                mod_mac(unit, ready, lambda k: head_rows[unit][:, k])

            def head_row(unit):
                dve.wait_ge(s_head_sum, unit - 1)
                if unit == 2:
                    dve.wait_ge(s_mod_row, 1)
                else:
                    dve.wait_ge(s_head_row, 1)
                dve.scalar_tensor_tensor(out=mod_rows[:], in0=ps[HEAD_BANK[unit]][0:ROWS, :],
                                         scalar=ident[0:ROWS, HEAD_ROW + unit:HEAD_ROW + unit + 1],
                                         in1=mod_rows[:], op0=ALU.mult, op1=ALU.add).then_inc(s_head_row, 1)

            dve.wait_ge(s_silu_c, 1)
            dve.wait_ge(s_const, 8)
            head_mac(0)
            mod_lo(0)
            mod_row(0)
            token_rstd(0)
            head_row(2)
            head_mac(1)
            mod_lo(1)
            head_row(3)
            dve.wait_ge(s_head_row, 2)
            mod_row(1)
            dve.wait_ge(s_vec_t, 1)
            dve.tensor_copy(vecs[:, KD:], ps[6][:, KD:64]).then_inc(s_vec, 1)
            V = NV * KD
            bm = ps[6][:, 64:64 + 2 * V].rearrange("p (l v k) -> p l v k", l=2, v=NV)
            bmv = bmod[:].rearrange("p l (v k) -> p l v k", v=NV)
            for v in range(NV):
                dve.tensor_scalar(bmv[:, :, v], bm[:, :, v], 1.0 if v % 3 == 1 else 0.0, None,
                                  ALU.add).then_inc(s_vec, 1)
            dve.tensor_copy(wdw[:], ps[6][:, 256:512].rearrange("p (k t) -> p k t", k=KD)[:, :, 0:TAPS]).then_inc(
                s_vec, 1)
            dve.wait_ge(s_vec, NV + 2)
            pair_lo(FIRST[FFA][0], 0, 0)
            mod_columns(0)
            normed(0, h, [(4, lambda: pair_lo(FIRST[FFA][1], 0, 1))])
            feed_forward(0, 1, (FIRST[FNET][0], PAIR[FNET]))

            def spectrum_lo(g):
                for t in range(TC):
                    dve.wait_ge(s_y_hi, TC * g + t + 1)
                    dve.tensor_tensor(y_lo[:, t], ps[t][:], y_hi[:, t].bitcast(F32), ALU.subtract).then_inc(s_y, 1)

            mod_columns(2)
            pair_lo(FIRST[FNET][1], PAIR[FNET], 1)
            token_rstd(1)
            normed(1, h, [(5, lambda: spectrum_lo(0)), (6, lambda: down_lo(TABLE_TAIL))])
            dve.tensor_copy(wdw_hi, wdw[:]).then_inc(s_wdw, 1)
            dve.wait_ge(s_wdw, 1)
            dve.tensor_tensor(wdw_lo[:], wdw[:], wdw_hi.bitcast(F32), ALU.subtract).then_inc(s_wdw, 1)
            add_mixer_bias(0, B_FNET)
            unit = HEAD + 2 + NI - 1
            for g in range(N_GROUPS):
                if g + 1 < N_GROUPS:
                    spectrum_lo(g + 1)
                for cc in range(2):
                    dve.wait_ge(s_f_hi, 2 * g + cc + 1)
                    dve.tensor_tensor(a_lo[:, 2 * g + cc], ps[SEQ_BANKS[g][cc]][:], a_hi[:, 2 * g + cc].bitcast(F32),
                                      ALU.subtract).then_inc(s_f, 1)
                if g == N_GROUPS - 2:
                    pair_lo(WO_UNITS[FNET][0], PAIR[FNET] + 1, 0)
                if 0 < g < N_GROUPS - 1:
                    mod_row(unit - 3)
                if g == N_GROUPS - 1:
                    pair_lo(WO_UNITS[FNET][1], PAIR[FNET] + 1, 1)
                    mod_lo(unit - 3)
                    pair_lo(WO_UNITS[FNET][2], PAIR[FNET] + 2, 0)
                mod_mac(unit - 2, mod_half_ready(16 * (unit - HEAD + 1)), ring_rows)
                if g < N_GROUPS - 2:
                    mod_lo(unit - 2)
                unit += 1
            project(2, 0, [(2, lambda: pair_lo(WO_UNITS[FNET][3], PAIR[FNET] + 2, 1)),
                           (5, lambda: pair_lo(FIRST[FFB][0], PAIR[FFB], 0))], unit)
            pair_lo(FIRST[FFB][1], PAIR[FFB], 1)
            mod_columns(3)
            token_rstd(2)
            normed(2, h)
            feed_forward(1, 3, (FIRST[FFC][0], PAIR[FFC]))
            mod_columns(4)
            pair_lo(FIRST[FFC][1], PAIR[FFC], 1)
            token_rstd(3)
            normed(3, h)
            feed_forward(2, 4, (FIRST[CONV][0], PAIR[CONV]))

            mod_columns(5)
            pair_lo(FIRST[CONV][1], PAIR[CONV], 1)
            token_rstd(4)
            normed(4, h)
            add_mixer_bias(1, B_OUT)
            for ch in range(KD + 1):
                if ch < KD:
                    dve.wait_ge(s_sig, ch + 1)
                    if ch >= 3:
                        dve.wait_ge(s_term, before(ch - 2, POOL_TAPS))
                    dve.scalar_tensor_tensor(out=u_pad[:, ch % 3, HALO:HALO + T], in0=ps[2 * (ch % 2)][:],
                                             scalar=vecs[:, B_IN + ch:B_IN + ch + 1], in1=tmp_a[:, ch % 2],
                                             op0=ALU.add, op1=ALU.mult).then_inc(s_u, 1)
                    dve.wait_ge(s_u_hi, ch + 1)
                    dve.tensor_tensor(u_lo[:, ch % 2], u_pad[:, ch % 3], u_hi[:, ch % 2].bitcast(F32),
                                      ALU.subtract).then_inc(s_u_lo, 1)
                    if ch + 2 < KD:
                        pair_lo(CONV_UNITS[ch + 2], PAIR[CONV] + (ch + 2) // 2, ch % 2)
                if ch == 0:
                    continue
                c1 = ch - 1
                apart = c1 == KD - 1
                bank = ps[4 + c1 % 2][:]
                even, odd = ps[MOD_BANK][:] if apart else bank, ps[6][:]
                taps = before(c1, DVE_TAPS)
                n_taps = len(DVE_TAPS[c1])
                for j, tap in enumerate(DVE_TAPS[c1]):
                    src, w = u_pad[:, c1 % 3, tap:tap + T], wdw[:, c1, tap:tap + 1]
                    if j == 0 and apart:
                        dve.tensor_scalar(even, src, w, None, ALU.mult).then_inc(s_tap, 1)
                        continue
                    acc = dst = even if j % 2 == 0 else odd
                    if j == 0:
                        dve.wait_ge(s_pe_tap, c1 + 1)
                    elif j == 1:
                        dve.wait_ge(s_pool_tap, before(c1 + 1, POOL_TAPS, 1))
                        acc = pool_acc[:, c1 % 2]
                    else:
                        dve.wait_ge(s_tap, taps + j - 1)
                    if j == n_taps - 1 - n_taps % 2:
                        dst = y_conv[:, c1]
                    dve.scalar_tensor_tensor(out=dst, in0=src, scalar=w, in1=acc, op0=ALU.mult,
                                             op1=ALU.add).then_inc(s_tap, 1)
                dve.wait_ge(s_tap, taps + n_taps)
                if apart:
                    dve.tensor_tensor(y_conv[:, c1], y_conv[:, c1], even, ALU.add).then_inc(s_merge, 1)
                    dve.wait_ge(s_merge, c1 + 1)
                    dve.wait_ge(s_pe_tap, c1 + 1)
                dve.tensor_tensor(y_conv[:, c1], y_conv[:, c1], bank, ALU.add).then_inc(s_merge, 1)
                if c1 >= 1:
                    dve.wait_ge(s_merge, c1 + 1 + apart)
                    if c1 >= 2:
                        dve.wait_ge(s_y_sum, c1 - 1)
                    dve.tensor_tensor(sq_sum[:], y_conv[:, 0] if c1 == 1 else sq_sum[:], y_conv[:, c1],
                                      ALU.add).then_inc(s_y_sum, 1)
            units = WO_UNITS[CONV]
            pair_lo(units[0], PAIR[CONV] + 4, 0)
            dve.wait_ge(s_mean, 1)
            for d in range(KD):
                dve.tensor_tensor(y_conv[:, d], y_conv[:, d], ps[MEAN_BANK][:],
                                  ALU.subtract).then_inc(s_center, 1)
                if d >= 1:
                    square_add(5, d - 1)
            square_add(5, KD - 1)
            token_rstd(5)
            normed(5, y_conv, [(3, lambda: pair_lo(units[1], PAIR[CONV] + 4, 1)),
                               (5, lambda: pair_lo(units[2], PAIR[CONV] + 5, 0))])
            project(6, 1, [(2, lambda: pair_lo(units[3], PAIR[CONV] + 5, 1)),
                           (5, lambda: pair_lo(FIRST[FFD][0], PAIR[FFD], 0))])
            pair_lo(FIRST[FFD][1], PAIR[FFD], 1)
            token_rstd(6)
            normed(6, h)
            feed_forward(3, None, None)
            for n in range(2 * TC):
                if n % 2 == 0:
                    dve.wait_ge(s_out_t, n + 1)
                    if n:
                        dve.wait_ge(s_out_row, n)
                    dve.tensor_copy(out_rows[0][:, n % TC, (n // TC) * 512:(n // TC + 1) * 512],
                                    ps[n][:]).then_inc(s_out_row, 1)

        @block.tensor
        def _(pe):
            def product(bank, wh, wl, xh, xl, start, stop):
                pe.matmul(bank, wh, xh, start=start, stop=False, skip_group_check=True)
                pe.matmul(bank, wl, xh, start=False, stop=False, skip_group_check=True)
                return pe.matmul(bank, wh, xl, start=False, stop=stop, skip_group_check=True)

            def mod_sum(unit):
                pe.wait_ge(s_mod_split, unit + 1)
                pe.matmul(ps[MOD_BANK][0:ROWS, :], ones_r[:], mod_acc_hi[:], start=True, stop=False,
                          skip_group_check=True)
                pe.matmul(ps[MOD_BANK][0:ROWS, :], ones_r[:], mod_acc_lo[:], start=False, stop=True,
                          skip_group_check=True).then_inc(s_mod_sum, 1)

            def mod_transpose(call):
                pe.wait_ge(s_mod_row, MOD_CALLS[call][1])
                bank = ps[MOD_T_BANK[call]]
                for j in range(UC):
                    ins = pe.transpose(bank[:, j * ROWS:(j + 1) * ROWS], mod_rows[:, j * P:(j + 1) * P],
                                       ident[0:ROWS, 0:ROWS])
                ins.then_inc(s_mod_t, 1)

            def head_sum(unit):
                for half in range(2):
                    pe.wait_ge(s_head_in[2 * unit + half], 16)
                    for k in range(4 * half, 4 * half + 4):
                        ins = pe.matmul(ps[HEAD_BANK[unit]][0:ROWS, :], silu_c[:, k:k + 1].to_broadcast([P, ROWS]),
                                        head_rows[unit][:, k], start=k == 0, stop=k == KD - 1)
                ins.then_inc(s_head_sum, 1)

            def token_sums(n):
                pe.wait_ge(s_sq_sum, ADDS * (n + 1))
                for t in range(TC):
                    ins = pe.matmul(ps[TOK_BANK][:, t:t + 1], sq_sum[:, t * P:(t + 1) * P], ones[:, 0:1],
                                    start=True, stop=True, skip_group_check=True)
                ins.then_inc(s_tok, 1)

            def spread_rstd(n):
                for t in range(TC):
                    pe.wait_ge(s_diag, TC * n + t + 1)
                    ins = pe.matmul(ps[RSTD_BANK][:, t * P:(t + 1) * P], ones[:], diag[:, t], start=True,
                                    stop=True, skip_group_check=True)
                ins.then_inc(s_rb, 1)

            def in_chunk(b, banks, n, waits_a, done):
                for k in range(KD):
                    if waits_a:
                        pe.wait_ge(s_a_hi, KD * n + k + 1)
                    for s in range(2):
                        tile_hi, tile_lo = w_hi[b][:, s * KD + k], w_lo[b][:, s * KD + k]
                        pe.matmul(ps[banks + s][:], tile_hi, a_hi[:, k], start=k == 0, stop=False,
                                  skip_group_check=True)
                        pe.matmul(ps[banks + s][:], tile_lo, a_hi[:, k], start=False, stop=False,
                                  skip_group_check=True)
                    if waits_a:
                        pe.wait_ge(s_a, KD * n + k + 1)
                    for s in range(2):
                        ins = pe.matmul(ps[banks + s][:], w_hi[b][:, s * KD + k], a_lo[:, k], start=False,
                                        stop=k == KD - 1, skip_group_check=True)
                ins.then_inc(done, 1)

            def up(f, i, ch, n, waits_a):
                b, use = UP[f][ch]
                pe.wait_ge(s_w[b], i + (use + 1))
                if not (isinstance(i, int) and i == 0):
                    pe.wait_ge(s_prod, i * 2 + (2 * NI * f + ch - 1))
                in_chunk(b, 2 * ch, n, waits_a, s_gu)

            def down(f, done, par, unit, last=False):
                b = DOWN_LAST[f][0] if last else DOWN[f][0]
                pe.wait_ge(s_w[b], DOWN_LAST[f][1] + 1 if last else done + (DOWN[f][1] + 1))
                pe.wait_ge(s_p, done * 2 + (2 * NI * f + 2))
                for d in range(KD):
                    if d >= 4:
                        pe.wait_ge(s_h, done * KD + (HB[FF_PHASE[f]] + d - 3))
                    else:
                        pe.wait_ge(s_h, done * KD + (HB[FF_PHASE[f]] + d - 3))
                    if d == 3 and unit is not None:
                        pe.wait_ge(s_mod_row, unit + 1)
                    for j in range(2):
                        ins = product(ps[4 + d % 4][:], w_hi[b][:, j * KD + d], w_lo[b][:, j * KD + d],
                                      p_hi[:, par, j], p_lo[:, par, j], j == 0, j == 1)
                    ins.then_inc(s_take, 1)

            def feed_forward(f, n):
                u0 = FF_UNIT0[f]
                up(f, 0, 0, n, True)
                up(f, 0, 1, n, False)
                if u0 is not None:
                    pe.wait_ge(s_mod_row, u0 - 2)
                    mod_sum(u0 - 2)

                def step(i, par, late_unit=False):
                    up(f, i, 0, n, False)
                    if late_unit:
                        pe.wait_ge(s_mod_row, u0 - 1)
                        mod_sum(u0 - 1)
                        if f == 0:
                            mod_transpose(1)
                    up(f, i, 1, n, False)
                    unit = None
                    if late_unit:
                        pe.wait_ge(s_mod_row, u0)
                    if f < 2:
                        unit = i + (u0 - 1)
                        if not late_unit:
                            pe.wait_ge(s_h, i * KD + (HB[FF_PHASE[f]] - KD))
                        mod_sum(unit)
                    down(f, i - 1, 1 - par, unit)

                step(1, 1, late_unit=u0 is not None)
                with pe.Fori(0, (NI - 3) // 2) as r:
                    for odd in range(2):
                        step(r * 2 + (2 + odd), odd)
                step(NI - 1, 0)
                down(f, NI - 1, 0, None, last=True)
                if f < 3:
                    mod_transpose(2 if f == 0 else 3 + f)

            def project(layer, uses, order_waits, n, unit=None):
                o = 0
                for j, (b, use) in enumerate(uses):
                    pe.wait_ge(s_w[b], use + 1)
                    for dd in range(2):
                        if o >= 4:
                            pe.wait_ge(s_h, NORM_H[n] + o - 3)
                        for k in range(KD):
                            if o == 0:
                                pe.wait_ge(*order_waits(k))
                            ins = product(ps[o % 4][:], w_hi[b][:, dd * KD + k], w_lo[b][:, dd * KD + k],
                                          a_hi[:, k], a_lo[:, k], k == 0, k == KD - 1)
                        ins.then_inc(s_take, 1)
                        o += 1
                    if unit is not None:
                        pe.wait_ge(s_mod_row, unit - 4 + j)
                        mod_sum(unit - 4 + j)

            pe.wait_ge(s_const, 8)
            pe.wait_ge(s_c_in, 16)
            pe.transpose(ps[MOD_BANK][:, C_COL:C_COL + KD], vec_rows[C_COL:C_COL + KD],
                         ident[0:KD, 0:KD]).then_inc(s_c_t, 1)
            pe.wait_ge(s_x_in, 16 * TC)
            for d in range(KD):
                if d >= 4:
                    pe.wait_ge(s_h, d - 3)
                for t in range(TC):
                    ins = pe.transpose(ps[d % 4][:, t * P:(t + 1) * P], x_rows[:, t, d * P:(d + 1) * P], ident[:])
                ins.then_inc(s_take, 1)
            pe.wait_ge(s_silu_c, 1)
            pe.wait_ge(s_h, KD)
            head_sum(2)
            mod_sum(0)
            token_sums(0)
            pe.wait_ge(s_vec_in, 16 * 8)
            pe.transpose(ps[6][:, 0:64], vec_rows, ident[0:64, 0:64])
            V = NV * KD
            for la in range(2):
                pe.transpose(ps[6][:, 64 + la * V:64 + (la + 1) * V], bmod_rows[:, la], ident[0:V, 0:V])
            for k in range(KD):
                ins = pe.transpose(ps[6][:, 256 + 32 * k:256 + 32 * k + TAPS], wdw_rows[:, k],
                                   ident[0:TAPS, 0:TAPS])
            ins.then_inc(s_vec_t, 1)
            spread_rstd(0)
            head_sum(3)
            pe.wait_ge(s_mod_row, 1)
            mod_sum(1)
            pe.wait_ge(s_head_row, 2)
            mod_transpose(0)
            feed_forward(0, 0)

            token_sums(1)
            spread_rstd(1)
            base = HEAD + 2 + NI - 1
            unit = base
            b_chan, b_seq = FIRST[FNET][0][0], (FIRST[FNET][1][0], TABLE_TAIL[0])
            pe.wait_ge(s_w[b_chan], FIRST[FNET][0][1] + 1)
            th = [w[b_chan][:].rearrange("p (z k a) n -> p z k (a n)", z=2, k=2)[:, 0] for w in (w_hi, w_lo)]

            def channel_dft(g):
                for t in range(TC):
                    if g > 0:
                        pe.wait_ge(s_y, TC * (g - 1) + t + 1)
                    for k in range(2):
                        if t == 0:
                            pe.wait_ge(s_a, KD + 2 * g + k + 1)
                        kk = 2 * g + k
                        tok = slice(t * P, (t + 1) * P)
                        ins = product(ps[t][:], a_hi[:, kk, tok], a_lo[:, kk, tok], th[0][:, k], th[1][:, k],
                                      k == 0, k == 1)
                    ins.then_inc(s_spec, 1)

            def sequence_dft(g):
                if g == N_GROUPS - 1:
                    pe.wait_ge(s_y, TC * g + SEQ_BANKS[g][1] + 1)
                elif g > 0:
                    pe.wait_ge(s_f, 2 * g)
                for t in range(TC):
                    if g == 0 and t % 2 == 0:
                        b, use = (FIRST[FNET][1], TABLE_TAIL)[t // 2]
                        pe.wait_ge(s_w[b], use + 1)
                    pe.wait_ge(s_y, TC * g + t + 1)
                    tabs = [w[b_seq[t // 2]][:].rearrange("p (t s a) n -> p t s (a n)", t=2, s=2)[:, t % 2]
                            for w in (w_hi, w_lo)]
                    for cc in range(2):
                        for s in range(2):
                            ch = slice(s * GW + cc * P, s * GW + (cc + 1) * P)
                            ins = product(ps[SEQ_BANKS[g][cc]][:], y_hi[:, t, ch], y_lo[:, t, ch], tabs[0][:, s],
                                          tabs[1][:, s], t == 0 and s == 0, t == TC - 1 and s == 1)
                    ins.then_inc(s_seq, 1)

            channel_dft(0)
            for g in range(N_GROUPS):
                if g + 1 < N_GROUPS:
                    channel_dft(g + 1)
                sequence_dft(g)
                if 0 < g < N_GROUPS - 1:
                    pe.wait_ge(s_mod_row, unit - 3)
                    mod_sum(unit - 3)
                unit += 1
            project(0, WO_UNITS[FNET], lambda k: (s_f, k + 1), 2, unit)
            pe.wait_ge(s_h, HB[FNET] + 5)
            mod_transpose(3)
            token_sums(2)
            spread_rstd(2)
            feed_forward(1, 2)
            token_sums(3)
            spread_rstd(3)
            feed_forward(2, 3)

            token_sums(4)
            spread_rstd(4)
            def conv_taps(ch):
                pe.wait_ge(s_u_lo, ch + 1)
                if ch >= 2:
                    pe.wait_ge(s_merge, ch - 1)
                n = len(PE_TAPS[ch])
                for j, tap in enumerate(PE_TAPS[ch]):
                    pe.wait_ge(s_diag_tap, before(ch, PE_TAPS) + j + 1)
                    tap_hi, tap_lo = tap_matrix(ch, j)
                    ins = product(ps[4 + ch % 2][:], tap_hi, tap_lo,
                                  u_hi[:, ch % 2, tap:tap + T], u_lo[:, ch % 2, tap:tap + T],
                                  j == 0, j == n - 1)
                ins.then_inc(s_pe_tap, 1)

            for ch in range(KD):
                b, use = CONV_UNITS[ch]
                pe.wait_ge(s_w[b], use + 1)
                if ch >= 2:
                    pe.wait_ge(s_u, ch - 1)
                in_chunk(b, 2 * (ch % 2), 4, ch == 0, s_cgu)
                if ch >= 1:
                    conv_taps(ch - 1)
            conv_taps(KD - 1)
            pe.wait_ge(s_y_sum, KD - 1)
            pe.matmul(ps[MEAN_BANK][:], mean_w[:], sq_sum[:], start=True, stop=True).then_inc(s_mean, 1)
            token_sums(5)
            spread_rstd(5)
            project(1, WO_UNITS[CONV], lambda k: (s_a, KD * 5 + k + 1), 6)
            token_sums(6)
            spread_rstd(6)
            feed_forward(3, 6)

            for n in range(2 * TC):
                if n == 0:
                    pe.wait_ge(s_h, HB[FFD] + KD * NI)
                for j in range(4):
                    d = (n // TC) * 4 + j
                    ins = pe.transpose(ps[n][:, j * P:(j + 1) * P], h[:, d, (n % TC) * P:(n % TC + 1) * P], ident[:])
                ins.then_inc(s_out_t, 1)


def dft_tables(T, D):
    gw = D // N_GROUPS
    kc = np.arange(gw)
    ang = 2 * np.pi * ((kc[:, None] * kc[None, :]) % gw) / gw
    chan = np.concatenate([np.cos(ang), np.sin(ang)], axis=1) / np.sqrt(gw)
    ks = np.arange(T)
    ang = 2 * np.pi * ((ks[:, None] * ks[None, :]) % T) / T
    seq = np.concatenate([np.cos(ang), -np.sin(ang)], axis=1) / np.sqrt(T)
    unit0 = np.zeros((P, 16, P))
    unit0[:, :8] = chan.reshape(2, P, 4, P).transpose(1, 0, 2, 3).reshape(P, 8, P)
    rows = seq.reshape(T // P, P, 2 * T).transpose(1, 0, 2)
    unit1 = rows[:, :2].reshape(P, 16, P)
    pair = np.stack([unit0, unit1], axis=2).reshape(P, -1)
    tail = rows[:, 2:].reshape(P, -1)
    return pair.astype(np.float32), tail.astype(np.float32)


_INS = ["x", "c", "w_mod", "b_mod", "w_ff_in", "w_ff_out", "fnet_w_out", "fnet_b_out", "conv_w_in", "conv_b_in",
        "conv_w_dw", "conv_b_dw", "conv_ln_g", "conv_ln_b", "conv_w_out", "conv_b_out"]


def kernel(**inputs):
    import concourse.bacc as _bacc
    from concourse.bass_utils import run_bass_kernel_spmd as _run

    nc = _bacc.Bacc("TRN2", target_bir_lowering=False, num_devices=1)
    arrays, args = {}, []

    def give(name, a):
        arrays[name] = a
        args.append(nc.dram_tensor(name, a.shape, mybir.dt.from_np(a.dtype), kind="ExternalInput").ap())

    for name in _INS:
        give(f"in_{name}", np.ascontiguousarray(inputs[name]))
    shape = inputs["x"].shape
    pair, tail = dft_tables(shape[1], shape[2])
    give("dft_pair", pair)
    give("dft_tail", tail)
    args.append(nc.dram_tensor("out_h", shape, F32, kind="ExternalOutput").ap())
    hybrid_backbone(nc, *args)
    r = _run(nc, [arrays], core_ids=[0])
    return r.results[0]["out_h"]
```
